# Optimizing a Trainium2 kernel written in Bass

```python
import math
import jax, jax.numpy as jnp
from jax import lax
import numpy as np

D_MODEL = 1024
BATCH = 1
SEQ = 256
DEPTH = 2

N_MEM = 256
EPS = 1e-6
NEG_INF = -1e30
Q_BLOCK = 128

DIFF_HEADS = 8
DIFF_QK_DIM = 64
DIFF_V_DIM = 2 * DIFF_QK_DIM
DIFF_QK_WIDTH = 2 * DIFF_HEADS * DIFF_QK_DIM
DIFF_WIDTH = DIFF_HEADS * DIFF_V_DIM

DIL_GROUPS = ((128, 1), (512, 4), (2048, 16))
N_DIL_GROUPS = len(DIL_GROUPS)
DIL_HEADS = 4
DIL_HEAD_DIM = 128
DIL_WIDTH = DIL_HEADS * DIL_HEAD_DIM
DIL_QKV_WIDTH = N_DIL_GROUPS * DIL_WIDTH

MEM_HEADS = 4
MEM_HEAD_DIM = 128
MEM_WIDTH = MEM_HEADS * MEM_HEAD_DIM

N_BRANCH = 3

REL_BUCKETS = 32
REL_MAX_DIST = 1024
N_BIAS_HEADS = DIFF_HEADS + N_DIL_GROUPS * DIL_HEADS

IN_SIZES = (DIFF_QK_WIDTH, DIFF_QK_WIDTH, DIFF_WIDTH, DIFF_WIDTH,
            DIL_QKV_WIDTH, DIL_QKV_WIDTH, DIL_QKV_WIDTH, DIL_WIDTH,
            MEM_WIDTH, MEM_WIDTH, N_BRANCH * D_MODEL)
N_IN = sum(IN_SIZES)


def rmsnorm(x, g=None):
    xf = x.astype(jnp.float32)
    y = xf * lax.rsqrt(jnp.mean(xf * xf, axis=-1, keepdims=True) + EPS)
    if g is not None:
        y = y * g.astype(jnp.float32)
    return y.astype(x.dtype)

def t5_bucket(rel):
    half = REL_BUCKETS // 2
    max_exact = half // 2
    ret = jnp.where(rel > 0, half, 0)
    n = jnp.abs(rel)
    nf = jnp.maximum(n, 1).astype(jnp.float32)
    large = max_exact + (jnp.log(nf / max_exact) / math.log(REL_MAX_DIST / max_exact)
                         * (half - max_exact)).astype(jnp.int32)
    large = jnp.minimum(large, half - 1)
    return ret + jnp.where(n < max_exact, n, large)

def diff_attention(q, k, v, lam, bias_tab):
    B, S = q.shape[0], q.shape[1]
    nq = S // Q_BLOCK
    scale = DIFF_QK_DIM ** -0.5
    qb = q.reshape(B, nq, Q_BLOCK, 2, DIFF_HEADS, DIFF_QK_DIM).transpose(1, 0, 2, 3, 4, 5)
    kpos = jnp.arange(S, dtype=jnp.int32)

    def one_block(args):
        qblk, i = args
        qpos = i * Q_BLOCK + jnp.arange(Q_BLOCK, dtype=jnp.int32)
        bias = bias_tab[t5_bucket(kpos[None, :] - qpos[:, None])]
        bias = jnp.transpose(bias, (2, 0, 1)).astype(jnp.float32)
        s = jnp.einsum('bqmhd,bkmhd->bmhqk', qblk, k,
                       preferred_element_type=jnp.float32) * scale + bias
        p = jax.nn.softmax(s, axis=-1)
        w = p[:, 0] - lam * p[:, 1]
        return jnp.einsum('bhqk,bkhe->bqhe', w.astype(v.dtype), v)

    out = lax.map(one_block, (qb, jnp.arange(nq, dtype=jnp.int32)))
    return out.transpose(1, 0, 2, 3, 4).reshape(B, S, DIFF_HEADS, DIFF_V_DIM)

def dilated_group(q, k, v, window, dilation, bias_tab):
    B, S, H, dh = q.shape
    r = dilation
    half = window // (2 * r)
    nb = half
    L = S // r
    nblk = -(-L // nb)
    Lp = nblk * nb
    Bn = B * r
    scale = dh ** -0.5

    def to_strided(t):
        return t.reshape(B, L, r, H, dh).transpose(0, 2, 1, 3, 4).reshape(Bn, L, H, dh)

    def band(t):
        tp = jnp.pad(t, ((0, 0), (nb, Lp - L + nb), (0, 0), (0, 0)))
        tp = tp.reshape(Bn, nblk + 2, nb, H, dh)
        return jnp.concatenate([tp[:, :-2], tp[:, 1:-1], tp[:, 2:]], axis=2)

    qs = jnp.pad(to_strided(q), ((0, 0), (0, Lp - L), (0, 0), (0, 0))).reshape(Bn, nblk, nb, H, dh)
    kb = band(to_strided(k))
    vb = band(to_strided(v))

    qi = jnp.arange(nb, dtype=jnp.int32)
    kj = jnp.arange(3 * nb, dtype=jnp.int32) - nb
    delta = kj[None, :] - qi[:, None]
    ksub = jnp.arange(nblk, dtype=jnp.int32)[:, None] * nb + kj[None, :]
    valid = (jnp.abs(delta) <= half)[None, :, :] & ((ksub >= 0) & (ksub < L))[:, None, :]
    bias = bias_tab[t5_bucket(delta * r)].astype(jnp.float32).transpose(2, 0, 1)

    s = jnp.einsum('bnqhd,bnkhd->bnhqk', qs, kb,
                   preferred_element_type=jnp.float32) * scale + bias
    s = jnp.where(valid[None, :, None], s, NEG_INF)
    m = jnp.max(s, axis=-1, keepdims=True)
    e = jnp.exp(s - m)
    den = jnp.sum(e, axis=-1, keepdims=True)
    o = jnp.einsum('bnhqk,bnkhd->bnqhd', (e / den).astype(v.dtype), vb)
    lse = (m + jnp.log(den))[..., 0]

    o = o.reshape(Bn, Lp, H, dh)[:, :L]
    lse = lse.transpose(0, 1, 3, 2).reshape(Bn, Lp, H)[:, :L]
    o = o.reshape(B, r, L, H, dh).transpose(0, 2, 1, 3, 4).reshape(B, S, H, dh)
    lse = lse.reshape(B, r, L, H).transpose(0, 2, 1, 3).reshape(B, S, H)
    return o, lse

def memory_attention(q, mk, mv):
    s = jnp.einsum('bshd,bmhd->bhsm', q, mk,
                   preferred_element_type=jnp.float32) * (MEM_HEAD_DIM ** -0.5)
    p = jax.nn.softmax(s, axis=-1)
    return jnp.einsum('bhsm,bmhd->bshd', p.astype(mv.dtype), mv)

def mixer_layer(x, mem, layer_idx, g_norm, w_in, lam_p, w_mem_kv, g_mem,
                w_br_diff, w_br_dil, w_br_mem, w_out, rel_bias):
    B, S, _ = x.shape
    h = rmsnorm(x, g_norm)
    z = jnp.einsum('bsd,dn->bsn', h, w_in)
    splits = np.cumsum(IN_SIZES)[:-1].tolist()
    dq, dk, dv, dg, lq, lk, lv, lg, mq, mg, mgate = jnp.split(z, splits, axis=-1)

    lam_init = 0.8 - 0.6 * math.exp(-0.3 * layer_idx)
    lp = lam_p.astype(jnp.float32)
    lam = jnp.exp(jnp.dot(lp[0], lp[1])) - jnp.exp(jnp.dot(lp[2], lp[3])) + lam_init
    o_a = diff_attention(dq.reshape(B, S, 2, DIFF_HEADS, DIFF_QK_DIM),
                         dk.reshape(B, S, 2, DIFF_HEADS, DIFF_QK_DIM),
                         dv.reshape(B, S, DIFF_HEADS, DIFF_V_DIM),
                         lam, rel_bias[:, :DIFF_HEADS])
    o_a = rmsnorm(o_a) * (1.0 - lam_init)
    y_a = jnp.einsum('bse,ed->bsd', o_a.reshape(B, S, DIFF_WIDTH) * jax.nn.silu(dg), w_br_diff)

    lq = lq.reshape(B, S, N_DIL_GROUPS, DIL_HEADS, DIL_HEAD_DIM)
    lk = lk.reshape(B, S, N_DIL_GROUPS, DIL_HEADS, DIL_HEAD_DIM)
    lv = lv.reshape(B, S, N_DIL_GROUPS, DIL_HEADS, DIL_HEAD_DIM)
    outs, lses = [], []
    for g, (window, dilation) in enumerate(DIL_GROUPS):
        c0 = DIFF_HEADS + g * DIL_HEADS
        o_g, lse_g = dilated_group(lq[:, :, g], lk[:, :, g], lv[:, :, g], window, dilation,
                                   rel_bias[:, c0:c0 + DIL_HEADS])
        outs.append(o_g.astype(jnp.float32))
        lses.append(lse_g)
    wts = jax.nn.softmax(jnp.stack(lses, axis=0), axis=0)
    o_b = jnp.einsum('gbsh,gbshe->bshe', wts, jnp.stack(outs, axis=0)).astype(x.dtype)
    y_b = jnp.einsum('bse,ed->bsd', o_b.reshape(B, S, DIL_WIDTH) * jax.nn.silu(lg), w_br_dil)

    mem_n = rmsnorm(mem, g_mem)
    kv = jnp.einsum('bmd,dn->bmn', mem_n, w_mem_kv).reshape(B, mem.shape[1], 2, MEM_HEADS, MEM_HEAD_DIM)
    o_m = memory_attention(mq.reshape(B, S, MEM_HEADS, MEM_HEAD_DIM), kv[:, :, 0], kv[:, :, 1])
    y_m = jnp.einsum('bse,ed->bsd', o_m.reshape(B, S, MEM_WIDTH) * jax.nn.silu(mg), w_br_mem)

    gates = jax.nn.sigmoid(mgate).reshape(B, S, N_BRANCH, D_MODEL)
    merged = gates[:, :, 0] * y_a + gates[:, :, 1] * y_b + gates[:, :, 2] * y_m
    return x + jnp.einsum('bsd,de->bse', merged, w_out)

def first_inputs(seed: int = 0) -> dict:
    key = jax.random.key(seed)
    ks = jax.random.split(key, 14)
    f32 = jnp.float32
    nrm = jax.random.normal
    return {
        'x': nrm(ks[0], (BATCH, SEQ, D_MODEL), f32),
        'mem': nrm(ks[1], (BATCH, N_MEM, D_MODEL), f32),
        'g_norm': 1.0 + 0.02 * nrm(ks[2], (DEPTH, D_MODEL), f32),
        'w_in': nrm(ks[3], (DEPTH, D_MODEL, N_IN), f32) * D_MODEL ** -0.5,
        'diff_lambda': 0.1 * nrm(ks[4], (DEPTH, 4, DIFF_QK_DIM), f32),
        'w_mem_kv': nrm(ks[5], (DEPTH, D_MODEL, 2 * MEM_WIDTH), f32) * D_MODEL ** -0.5,
        'g_mem': 1.0 + 0.02 * nrm(ks[6], (DEPTH, D_MODEL), f32),
        'w_br_diff': nrm(ks[7], (DEPTH, DIFF_WIDTH, D_MODEL), f32) * DIFF_WIDTH ** -0.5,
        'w_br_dil': nrm(ks[8], (DEPTH, DIL_WIDTH, D_MODEL), f32) * DIL_WIDTH ** -0.5,
        'w_br_mem': nrm(ks[9], (DEPTH, MEM_WIDTH, D_MODEL), f32) * MEM_WIDTH ** -0.5,
        'w_out': nrm(ks[10], (DEPTH, D_MODEL, D_MODEL), f32) * D_MODEL ** -0.5,
        'rel_bias': 0.2 * nrm(ks[11], (REL_BUCKETS, N_BIAS_HEADS), f32),
        'g_final': 1.0 + 0.02 * nrm(ks[12], (D_MODEL,), f32),
    }

def first_block(x, mem, g_norm, w_in, diff_lambda, w_mem_kv, g_mem,
              w_br_diff, w_br_dil, w_br_mem, w_out, rel_bias, g_final):
    for l in range(DEPTH):
        x = mixer_layer(x, mem, l, g_norm[l], w_in[l], diff_lambda[l], w_mem_kv[l], g_mem[l],
                        w_br_diff[l], w_br_dil[l], w_br_mem[l], w_out[l], rel_bias)
    return rmsnorm(x, g_final)


DEPTH_2 = 4

N_MIXERS = 3
HEAD_DIM = 64
RMS_EPS = 1e-6
SWA_Q_HEADS = D_MODEL // HEAD_DIM
SWA_KV_HEADS = SWA_Q_HEADS // 4
SWA_WINDOW = 128
ROPE_THETA = 150000.0
GLA_HEADS = 4
GLA_DK = D_MODEL // 2
GLA_DV = D_MODEL
GLA_RANK = 16
GLA_TAU = 16.0
GLA_CHUNK = 64
FOX_HEADS = D_MODEL // HEAD_DIM
FOX_BLOCK = 128
D_FF = -(-8 * D_MODEL // (3 * 256)) * 256


def rmsnorm_2(x, g):
    xf = x.astype(jnp.float32)
    y = xf * lax.rsqrt(jnp.mean(xf * xf, axis=-1, keepdims=True) + RMS_EPS)
    return (y * g.astype(jnp.float32)).astype(x.dtype)

def modulate(h, shift, scale):
    return h * (1 + scale[:, None, :]) + shift[:, None, :]

def rope(x, pos):
    hd = x.shape[-1]
    inv = 1.0 / (ROPE_THETA ** (jnp.arange(0, hd, 2, dtype=jnp.float32) / hd))
    ang = pos[:, None] * inv[None, :]
    cos = jnp.cos(ang)[None, :, None, :]
    sin = jnp.sin(ang)[None, :, None, :]
    xf = x.astype(jnp.float32)
    x1, x2 = jnp.split(xf, 2, axis=-1)
    return jnp.concatenate([x1 * cos - x2 * sin, x2 * cos + x1 * sin], axis=-1).astype(x.dtype)

def swa_mixer(h, w_in, sinks, w_o):
    B, S, _ = h.shape
    W, hd, Hq, Hkv = SWA_WINDOW, HEAD_DIM, SWA_Q_HEADS, SWA_KV_HEADS
    G = Hq // Hkv
    nb = S // W
    proj = h @ w_in
    q, k, v = jnp.split(proj, [Hq * hd, (Hq + Hkv) * hd], axis=-1)
    pos = jnp.arange(S, dtype=jnp.float32)
    q = rope(q.reshape(B, S, Hq, hd), pos)
    k = rope(k.reshape(B, S, Hkv, hd), pos)
    v = v.reshape(B, S, Hkv, hd)
    qb = q.reshape(B, nb, W, Hkv, G, hd)
    kb = k.reshape(B, nb, W, Hkv, hd)
    vb = v.reshape(B, nb, W, Hkv, hd)
    pad = ((0, 0), (1, 0), (0, 0), (0, 0), (0, 0))
    kk = jnp.concatenate([jnp.pad(kb, pad)[:, :-1], kb], axis=2)
    vv = jnp.concatenate([jnp.pad(vb, pad)[:, :-1], vb], axis=2)
    scores = jnp.einsum('bnqkgd,bnskd->bnkgqs', qb, kk).astype(jnp.float32) * (hd ** -0.5)
    i = jnp.arange(W)[:, None]
    j = jnp.arange(2 * W)[None, :]
    diff = i - j + W
    band = (diff >= 0) & (diff < W)
    has_prev = (jnp.arange(nb) > 0)[:, None, None] | (j >= W)[None]
    mask = band[None] & has_prev
    scores = jnp.where(mask[None, :, None, None], scores, -jnp.inf)
    sink_col = jnp.broadcast_to(
        sinks.astype(jnp.float32).reshape(Hkv, G)[None, None, :, :, None, None],
        scores.shape[:-1] + (1,))
    probs = jax.nn.softmax(jnp.concatenate([scores, sink_col], axis=-1), axis=-1)[..., :-1]
    out = jnp.einsum('bnkgqs,bnskd->bnqkgd', probs.astype(vv.dtype), vv)
    return out.reshape(B, S, Hq * hd) @ w_o

def gla_chunk_step(state, inp):
    q, k, v, b = inp
    C = q.shape[2]
    causal = jnp.tril(jnp.ones((C, C), dtype=bool))
    diff = b[:, :, :, None, :] - b[:, :, None, :, :]
    decay = jnp.exp(jnp.where(causal[None, None, :, :, None], diff, -jnp.inf))
    attn = jnp.einsum('bhtd,bhsd,bhtsd->bhts', q, k, decay)
    o = attn @ v + jnp.einsum('bhtd,bhde->bhte', q * jnp.exp(b), state)
    b_last = b[:, :, -1:, :]
    state = jnp.exp(b_last[:, :, 0, :])[..., None] * state + \
        jnp.einsum('bhsd,bhse->bhde', k * jnp.exp(b_last - b), v)
    return state, o

def gla_mixer(h, w_in, w_gate_up, b_gate, head_norm, w_o):
    B, S, _ = h.shape
    H, C = GLA_HEADS, GLA_CHUNK
    dk, dv = GLA_DK // H, GLA_DV // H
    nc = S // C
    proj = h @ w_in
    q, k, v, r, a_low = jnp.split(
        proj, [GLA_DK, 2 * GLA_DK, 2 * GLA_DK + GLA_DV, 2 * GLA_DK + 2 * GLA_DV], axis=-1)
    log_alpha = jax.nn.log_sigmoid((a_low @ w_gate_up + b_gate).astype(jnp.float32)) / GLA_TAU

    def to_chunks(t, d):
        return t.astype(jnp.float32).reshape(B, nc, C, H, d).transpose(1, 0, 3, 2, 4)

    qc = to_chunks(q, dk) * (dk ** -0.5)
    kc = to_chunks(k, dk)
    vc = to_chunks(v, dv)
    bc = jnp.cumsum(to_chunks(log_alpha, dk), axis=3)
    state0 = jnp.zeros((B, H, dk, dv), jnp.float32)
    _, o = lax.scan(gla_chunk_step, state0, (qc, kc, vc, bc))
    o = o.transpose(1, 0, 3, 2, 4).reshape(B, S, H, dv).astype(h.dtype)
    o = rmsnorm_2(o, head_norm)
    o = o * jax.nn.silu(r).reshape(B, S, H, dv)
    return o.reshape(B, S, GLA_DV) @ w_o

def fox_mixer(h, w_in, b_f, w_o):
    B, S, D = h.shape
    H, hd, blk = FOX_HEADS, HEAD_DIM, FOX_BLOCK
    proj = h @ w_in
    q, k, v, f_logit = jnp.split(proj, [D, 2 * D, 3 * D], axis=-1)
    log_f = jax.nn.log_sigmoid(f_logit.astype(jnp.float32) + b_f.astype(jnp.float32))
    lc = jnp.cumsum(log_f, axis=1).transpose(0, 2, 1)
    q = q.reshape(B, S, H, hd).transpose(0, 2, 1, 3)
    k = k.reshape(B, S, H, hd).transpose(0, 2, 1, 3)
    v = v.reshape(B, S, H, hd).transpose(0, 2, 1, 3)
    outs = []
    for i in range(S // blk):
        t0, t1 = i * blk, (i + 1) * blk
        s = jnp.einsum('bhqd,bhkd->bhqk', q[:, :, t0:t1], k[:, :, :t1]).astype(jnp.float32) * (hd ** -0.5)
        s = s + lc[:, :, t0:t1, None] - lc[:, :, None, :t1]
        mask = jnp.arange(t1)[None, :] <= (t0 + jnp.arange(blk))[:, None]
        p = jax.nn.softmax(jnp.where(mask[None, None], s, -jnp.inf), axis=-1)
        outs.append(jnp.einsum('bhqk,bhkd->bhqd', p.astype(v.dtype), v[:, :, :t1]))
    o = jnp.concatenate(outs, axis=2).transpose(0, 2, 1, 3).reshape(B, S, D)
    return o @ w_o

def swiglu(h, w_gu, w_down):
    g, u = jnp.split(h @ w_gu, 2, axis=-1)
    return (jax.nn.silu(g) * u) @ w_down

def second_inputs(seed: int = 0) -> dict:
    key = jax.random.key(seed)
    ks = iter(jax.random.split(key, 32))
    D = D_MODEL
    n_swa, n_gla, n_fox = (DEPTH_2 + 2) // 3, (DEPTH_2 + 1) // 3, DEPTH_2 // 3
    nrm = lambda k, shape, s: s * jax.random.normal(k, shape, jnp.float32)
    swa_cols = (SWA_Q_HEADS + 2 * SWA_KV_HEADS) * HEAD_DIM
    gla_cols = 2 * GLA_DK + 2 * GLA_DV + GLA_RANK
    fox_cols = 3 * D + FOX_HEADS
    return {
        "x": nrm(next(ks), (BATCH, SEQ, D), 1.0),
        "c": nrm(next(ks), (BATCH, D), 1.0),
        "ada_w": nrm(next(ks), (DEPTH_2, D, 6 * D), 0.5 * D ** -0.5),
        "ada_b": nrm(next(ks), (DEPTH_2, 6 * D), 0.02),
        "norm_gain": 1.0 + nrm(next(ks), (DEPTH_2, 2, D), 0.05),
        "ffn_w_gu": nrm(next(ks), (DEPTH_2, D, 2 * D_FF), D ** -0.5),
        "ffn_w_down": nrm(next(ks), (DEPTH_2, D_FF, D), D_FF ** -0.5),
        "swa_w_in": nrm(next(ks), (n_swa, D, swa_cols), D ** -0.5),
        "swa_sinks": nrm(next(ks), (n_swa, SWA_Q_HEADS), 0.5),
        "swa_w_o": nrm(next(ks), (n_swa, SWA_Q_HEADS * HEAD_DIM, D), (SWA_Q_HEADS * HEAD_DIM) ** -0.5),
        "gla_w_in": nrm(next(ks), (n_gla, D, gla_cols), D ** -0.5),
        "gla_w_gate_up": nrm(next(ks), (n_gla, GLA_RANK, GLA_DK), GLA_RANK ** -0.5),
        "gla_b_gate": nrm(next(ks), (n_gla, GLA_DK), 0.1),
        "gla_head_norm": 1.0 + nrm(next(ks), (n_gla, GLA_DV // GLA_HEADS), 0.05),
        "gla_w_o": nrm(next(ks), (n_gla, GLA_DV, D), GLA_DV ** -0.5),
        "fox_w_in": nrm(next(ks), (n_fox, D, fox_cols), D ** -0.5),
        "fox_b_f": jax.random.uniform(next(ks), (n_fox, FOX_HEADS), jnp.float32, 0.0, 3.0),
        "fox_w_o": nrm(next(ks), (n_fox, D, D), D ** -0.5),
        "final_norm": 1.0 + nrm(next(ks), (D,), 0.05),
    }

def second_block(x, c, ada_w, ada_b, norm_gain, ffn_w_gu, ffn_w_down,
              swa_w_in, swa_sinks, swa_w_o,
              gla_w_in, gla_w_gate_up, gla_b_gate, gla_head_norm, gla_w_o,
              fox_w_in, fox_b_f, fox_w_o, final_norm):
    c_act = jax.nn.silu(c)
    for i in range(DEPTH_2):
        kind, j = i % N_MIXERS, i // N_MIXERS
        mod = c_act @ ada_w[i] + ada_b[i]
        sh1, sc1, g1, sh2, sc2, g2 = jnp.split(mod, 6, axis=-1)
        h = modulate(rmsnorm_2(x, norm_gain[i, 0]), sh1, sc1)
        if kind == 0:
            y = swa_mixer(h, swa_w_in[j], swa_sinks[j], swa_w_o[j])
        elif kind == 1:
            y = gla_mixer(h, gla_w_in[j], gla_w_gate_up[j], gla_b_gate[j], gla_head_norm[j], gla_w_o[j])
        else:
            y = fox_mixer(h, fox_w_in[j], fox_b_f[j], fox_w_o[j])
        x = x + g1[:, None, :] * y
        h = modulate(rmsnorm_2(x, norm_gain[i, 1]), sh2, sc2)
        x = x + g2[:, None, :] * swiglu(h, ffn_w_gu[i], ffn_w_down[i])
    return rmsnorm_2(x, final_norm)


def setup_inputs(seed=0):
    out = dict(first_inputs(seed))
    for name, value in second_inputs(seed + 1).items():
        if name != "x":
            out[name + "_2"] = value
    return out


def reference(
    x, mem, g_norm, w_in, diff_lambda, w_mem_kv, g_mem, w_br_diff, w_br_dil, w_br_mem, w_out,
    rel_bias, g_final, c_2, ada_w_2, ada_b_2, norm_gain_2, ffn_w_gu_2, ffn_w_down_2, swa_w_in_2,
    swa_sinks_2, swa_w_o_2, gla_w_in_2, gla_w_gate_up_2, gla_b_gate_2, gla_head_norm_2,
    gla_w_o_2, fox_w_in_2, fox_b_f_2, fox_w_o_2, final_norm_2,
):
    x = first_block(
        x, mem, g_norm, w_in, diff_lambda, w_mem_kv, g_mem, w_br_diff, w_br_dil, w_br_mem,
        w_out, rel_bias, g_final,
    )
    return second_block(
        x, c_2, ada_w_2, ada_b_2, norm_gain_2, ffn_w_gu_2, ffn_w_down_2, swa_w_in_2,
        swa_sinks_2, swa_w_o_2, gla_w_in_2, gla_w_gate_up_2, gla_b_gate_2, gla_head_norm_2,
        gla_w_o_2, fox_w_in_2, fox_b_f_2, fox_w_o_2, final_norm_2,
    )


_drawn_inputs = setup_inputs


def setup_inputs(seed=0):
    import zlib

    import numpy as np

    out = dict(_drawn_inputs(seed))
    spreads = {}
    factors = {'g_norm': 3.313,
     'g_mem': 8.0,
     'swa_sinks_2': 8.0,
     'gla_b_gate_2': 5.036,
     'gla_head_norm_2': 5.271}
    for name, (base, spread) in spreads.items():
        noise = np.random.default_rng([zlib.crc32(name.encode()), seed]).standard_normal(out[name].shape)
        drawn = base * np.exp(spread * noise) if base else spread * noise
        out[name] = __import__('jax').numpy.asarray(drawn.astype(out[name].dtype))
    for name, factor in factors.items():
        out[name] = (out[name] * factor).astype(out[name].dtype)
    return out
```

```python
import math
from contextlib import ExitStack

import numpy as np
import concourse.bass as bass
from concourse import mybir

F32 = mybir.dt.float32
F32R = mybir.dt.float32r
ALU = mybir.AluOpType
ACT = mybir.ActivationFunctionType
AXX = mybir.AxisListType.X

P = 128
D = 1024
T = 256
N_IN = 13312
DFF = 2816
EPS = 1e-6
OFF = dict(dq=0, dk=1024, dv=2048, dg=3072, lq=4096, lk=5632, lv=7168, lg=8704, mq=9216, mg=9728,
           mgate=10240)
NEG = -1e30


def bucket(rel):
    half, max_exact = 16, 8
    ret = np.where(rel > 0, half, 0)
    n = np.abs(rel)
    nf = np.maximum(n, 1).astype(np.float32)
    large = max_exact + (np.log(nf / np.float32(max_exact)) / np.float32(math.log(1024 / max_exact))
                         * np.float32(half - max_exact)).astype(np.int32)
    return ret + np.where(n < max_exact, n, np.minimum(large, half - 1))


def constants():
    c = {}
    i = np.arange(P)
    c["ident"] = np.eye(P, dtype=np.float32)
    rel = np.arange(512) - 255
    oh = (bucket(rel)[None, :] == np.arange(32)[:, None]).astype(np.float32)
    c["onehot"] = oh
    dm = np.zeros((20, 512), np.float32)
    dm[8:12] = np.where(np.abs(rel) <= 64, 0, NEG)
    dm[12:16] = np.where(rel % 4 == 0, 0, NEG)
    dm[16:20] = np.where(rel % 16 == 0, 0, NEG)
    c["dilmask"] = dm
    inv = (1.0 / (np.float32(150000.0) ** (np.arange(0, 64, 2, dtype=np.float32) / np.float32(64)))
           ).astype(np.float32)
    ang = np.arange(T, dtype=np.float32)[:, None] * inv[None, :]
    cos, sin = np.cos(ang).astype(np.float32), np.sin(ang).astype(np.float32)
    cs = np.stack([np.concatenate([cos, cos], 1), np.concatenate([-sin, sin], 1)])
    c["rope"] = np.ascontiguousarray(cs.reshape(2, 2, P, 64).transpose(2, 0, 1, 3)).reshape(P, 256)
    tri = np.where(i[None, :] <= i[:, None], 0, NEG).astype(np.float32)
    prev = np.where(i[None, :] > i[:, None], 0, NEG).astype(np.float32)
    c["swamask"] = np.concatenate([prev, tri], 1)
    c["foxmask"] = np.concatenate([np.zeros((P, P), np.float32), tri], 1)
    dl = np.zeros((P, 9, P), np.float32)
    mk = np.zeros((P, 8, P), np.float32)
    for l in range(7):
        h = 64 >> l
        for t in range(P):
            mid = t // (2 * h) * 2 * h + h
            if t >= mid:
                dl[mid:t + 1, l, t] = 1
                mk[mid - h:mid, l, t] = 1
            else:
                dl[t + 1:mid, l, t] = 1
    dl[:, 7, :] = i[:, None] > i[None, :]
    dl[:, 8, :] = i[:, None] <= i[None, :]
    mk[:, 7, :] = np.eye(P)
    c["gladec"] = (dl / 16).reshape(P, 9 * P)
    c["glamask"] = (mk * np.float32(128 ** -0.5)).reshape(P, 8 * P)
    j = np.arange(T)
    up = (j[:, None] <= j[None, :]).astype(np.float32)
    c["cum"] = np.ascontiguousarray(up.reshape(2, P, T).transpose(1, 0, 2)).reshape(P, 512)
    return {k: np.ascontiguousarray(v, dtype=np.float32) for k, v in c.items()}


class Q:

    def __init__(self, key):
        self.key, self.n, self.ops, self.seen = key, 0, [], {}

    def wait(self, *toks):
        for t in toks:
            if t is None:
                continue
            if isinstance(t, list):
                self.wait(*t)
                continue
            k, v = t
            if self.seen.get(k, 0) < v:
                self.seen[k] = v
                self.ops.append(("wait", k, v))

    def do(self, fn, *waits, inc=True):
        self.wait(*waits)
        self.ops.append(("do", fn, inc))
        if inc:
            self.n += 1
            return (self.key, self.n)
        return None

    def dma(self, out, in_, key, count, *waits):
        self.wait(*waits)
        self.ops.append(("dma", out, in_, key))
        return (key, count)

    def mm(self, out, lhsT, rhs, start, stop, *waits, inc=False, skip=False):
        return self.do(lambda e: e.matmul(out, lhsT, rhs, start=start, stop=stop, skip_group_check=skip),
                       *waits, inc=inc)

    def tr(self, out, in_, ident, *waits, inc=False):
        return self.do(lambda e: e.transpose(out, in_, ident), *waits, inc=inc)

    def act(self, out, in_, func, *waits, bias=0.0, scale=1.0, accum=None):
        return self.do(lambda e: e.activation(out, in_, func, bias=bias, scale=scale, accum_out=accum), *waits)

    def copy(self, out, in_, *waits):
        return self.do(lambda e: e.tensor_copy(out, in_), *waits)

    def tt(self, out, a, b, op, *waits):
        return self.do(lambda e: e.tensor_tensor(out, a, b, op), *waits)

    def ts(self, out, a, s1, s2, op0, op1, *waits):
        if s2 is None:
            return self.do(lambda e: e.tensor_scalar(out, a, s1, None, op0), *waits)
        return self.do(lambda e: e.tensor_scalar(out, a, s1, s2, op0, op1), *waits)

    def stt(self, out, a, s, b, op0, op1, *waits):
        return self.do(lambda e: e.scalar_tensor_tensor(out=out, in0=a, scalar=s, in1=b, op0=op0, op1=op1), *waits)

    def red(self, out, in_, op, *waits, negate=False):
        return self.do(lambda e: e.tensor_reduce(out, in_, AXX, op, negate=negate), *waits)

    def recip(self, out, in_, *waits):
        return self.do(lambda e: e.reciprocal(out, in_), *waits)

    def memset(self, ap, v, *waits):
        return self.do(lambda e: e.memset(ap, v), *waits)


ORD = (0, 2, 1, 3)
NRAW = 6
NSPL = 5
LOOK = 3


def program(nc, I, C, out):
    pe, sc, ve, po, sp = Q("pe"), Q("sc"), Q("ve"), Q("po"), Q("sp")
    with ExitStack() as ctx:
        def sb(name, shape, dt=F32):
            return ctx.enter_context(nc.sbuf_tensor(name, shape, dt))

        sems = {k: ctx.enter_context(nc.semaphore("s_" + k)) for k in ("pe", "sc", "ve", "po")}

        def sem(name):
            sems[name] = ctx.enter_context(nc.semaphore("s_" + name))
            return name

        raw = sb("raw", [P, NRAW, 4, 512])
        whi = sb("whi", [P, NSPL, 2, 512], F32R)
        wlo = sb("wlo", [P, NSPL, 2, 512], F32R)
        X = sb("X", [P, 2, D])

        class TA:

            def __init__(self, n):
                self.hi = sb(n + "h", [P, 8, T], F32R)
                self.lo = sb(n + "l", [P, 8, T], F32R)
                self.tok = [[] for _ in range(8)]
                self.free = [[] for _ in range(8)]

            def write(self, b0, nb, toks):
                for b in range(b0, b0 + nb):
                    self.tok[b] = toks

            def waits(self, b0, nb):
                return [t for b in range(b0, b0 + nb) for t in self.free[b]]

        HT, OT = TA("HT"), TA("OT")
        NB = 45
        pool = sb("pool", [P, NB, 256])
        bias_t = sb("bias_t", [P, 6, 384])
        ident = sb("ident_t", [P, P])
        cols = sb("cols", [P, P])
        adb = sb("adb", [P, 192])
        mod = sb("mod", [P, 192])
        SM = 320
        sm = sb("sm", [P, SM])
        c8 = sb("c8", [P, 8])
        ones = sb("ones", [P, 1])
        mhalf = sb("mhalf", [P, 16])
        nlam = sb("nlam", [P, 2])
        w16h = sb("w16h", [P, 8, 16], F32R)
        w16l = sb("w16l", [P, 8, 16], F32R)
        scratch = nc.dram_tensor("bias_scratch", (20, P, 512), F32, kind="Internal").ap()

        GB = [ctx.enter_context(nc.psum_tensor(f"G{i}", [P, 512], F32)) for i in range(4)]
        AB = [ctx.enter_context(nc.psum_tensor(f"A{i}", [P, 2, 512], F32)) for i in range(2)]

        class Slot:
            def __init__(self, j):
                self.j, self.ps, self.ps_free = j, AB[j], []
                self.S, self.S_free = sb(f"S{j}", [P, 1040]), []
                self.W, self.W_free = sb(f"W{j}", [P, 1536]), []

        slots = [Slot(0), Slot(1)]

        gfree = [[] for _ in range(4)]
        gnext = [0]

        def gbank():
            g = gnext[0] % 4
            gnext[0] += 1
            return g

        pfree = [[] for _ in range(NB)]
        pbusy = [False] * NB

        class Blk:

            def __init__(self, n):
                for k in range(NB - n + 1):
                    if not any(pbusy[k:k + n]):
                        break
                else:
                    raise MemoryError(f"pool: {n} wanted, busy {sum(pbusy)}")
                self.k, self.n = k, n
                self.w = [t for j in range(k, k + n) for t in pfree[j]]
                pbusy[k:k + n] = [True] * n
                self.a = pool[:, k:k + n, :].rearrange("p n c -> p (n c)")
                self.tok = []

            def release(self, toks):
                for j in range(self.k, self.k + self.n):
                    pbusy[j] = False
                    pfree[j] = list(toks)

        def can(n):
            return pbusy.count(False) >= n

        smn = [0]

        def smc(n):
            if smn[0] % SM + n > SM:
                smn[0] += SM - smn[0] % SM
            a = smn[0] % SM
            smn[0] += n
            return sm[:, a:a + n]

        pend, live = [], [None, None]

        def step():
            for j in range(2):
                if live[j] is None and pend:
                    live[j] = pend.pop(0)(slots[j])
                if live[j] is not None:
                    try:
                        next(live[j])
                    except StopIteration:
                        live[j] = None

        def busy():
            return bool(pend) or live[0] is not None or live[1] is not None

        def mk_blk(n):
            while True:
                fits = any(not any(pbusy[k:k + n]) for k in range(NB - n + 1))
                if fits and (pbusy.count(False) >= n + 4 or not busy()):
                    return Blk(n)
                if not busy():
                    raise MemoryError(f"{n} of " + "".join("#" if b else "." for b in pbusy))
                step()

        def drain(cond):
            while not cond():
                if not busy():
                    raise MemoryError("".join("#" if b else "." for b in pbusy))
                step()

        def cseg(w, r0, nk, segs):
            res, at = [], 0
            for c0, n in segs:
                res.append((at, n, w[r0:r0 + nk * P, c0:c0 + n].rearrange("(c p) n -> p c n", p=P)))
                at += n
            return res

        def unit(key, w, K, segs):
            return [("w", key, cseg(w, k * 512, 4, segs)) for k in range(K // 512)]

        def plan():
            for l in range(2):
                wi = I["w_in"][l]
                for u in range(2):
                    yield from unit(("mkv", l, u), I["w_mem_kv"][l], D, [(u * 512, 512)])
                yield from unit(("mq", l), wi, D, [(OFF["mq"], 512)])
                yield from unit(("mg", l), wi, D, [(OFF["mg"], 512)])
                for pr in range(2):
                    def g(o, gi):
                        return (OFF[o] + gi * 512 + pr * 256, 256)
                    yield from unit(("dil", l, pr, 0), wi, D, [g("lq", 0), g("lq", 1)])
                    yield from unit(("dil", l, pr, 1), wi, D, [g("lq", 2), g("lk", 2)])
                    yield from unit(("dil", l, pr, 2), wi, D, [g("lk", 0), g("lk", 1)])
                    yield from unit(("dil", l, pr, 3), wi, D, [g("lv", 0), g("lv", 1)])
                    yield from unit(("dil", l, pr, 4), wi, D, [g("lv", 2), (OFF["lg"] + pr * 256, 256)])
                for u in range(2):
                    yield from unit(("gate", l, 2, u), wi, D, [(OFF["mgate"] + 2048 + u * 512, 512)])
                    yield from unit(("ym", l, u), I["w_br_mem"][l], 512, [(u * 512, 512)])
                for hf in range(2):
                    yield from unit(("diff", l, hf, 0), wi, D, [(hf * 256, 256), (512 + hf * 256, 256)])
                    yield from unit(("diff", l, hf, 1), wi, D,
                                    [(1024 + hf * 256, 256), (1536 + hf * 256, 256)])
                    yield from unit(("diff", l, hf, 2), wi, D, [(2048 + hf * 512, 512)])
                    yield from unit(("diff", l, hf, 3), wi, D, [(3072 + hf * 512, 512)])
                for u in range(2):
                    yield from unit(("gate", l, 1, u), wi, D, [(OFF["mgate"] + 1024 + u * 512, 512)])
                    yield from unit(("yb", l, u), I["w_br_dil"][l], 512, [(u * 512, 512)])
                for u in range(2):
                    yield from unit(("gate", l, 0, u), wi, D, [(OFF["mgate"] + u * 512, 512)])
                for u in range(2):
                    yield from unit(("ya", l, u), I["w_br_diff"][l], D, [(u * 512, 512)])
                for u in range(2):
                    yield from unit(("wo", l, u), I["w_out"][l], D, [(u * 512, 512)])
            for l in range(4):
                kind, j = l % 3, l // 3
                if kind == 0:
                    for u in (2, 0, 1):
                        yield from unit(("swa", l, u), I["swa_w_in_2"][j], D, [(u * 512, 512)])
                    wo = I["swa_w_o_2"][j]
                elif kind == 1:
                    for u in range(6):
                        yield from unit(("gla", l, u), I["gla_w_in_2"][j], D, [(u * 512, 512)])
                    wo = I["gla_w_o_2"][j]
                else:
                    for u in (0, 2, 4, 1, 3, 5):
                        yield from unit(("fox", l, u), I["fox_w_in_2"][j], D, [(u * 512, 512)])
                    wo = I["fox_w_o_2"][j]
                for u in range(2):
                    yield from unit(("wo2", l, u), wo, D, [(u * 512, 512)])
                for u in range(12):
                    if u < 11:
                        yield from unit(("gu", l, u), I["ffn_w_gu_2"][l], D, [(u * 256, 256), (DFF + u * 256, 256)])
                    if u > 0:
                        v = u - 1
                        wd = I["ffn_w_down_2"][l][v * 256:v * 256 + 256, :]
                        yield ("w", ("dn", l, v), [("dn", 0, wd.rearrange("(c p) n -> p c n", p=P))])

        def full_plan():
            ada = [("ada", (l, u, k), cseg(I["ada_w_2"][l], k * 512, 4, [(u * 512, 512)]))
                   for l in range(4) for u in range(12) for k in range(2)]
            main = list(plan())
            n1 = sum(1 for m in main if m[1][0] in FIRST)
            first, at, gave = 6, 0, 0
            for i, m in enumerate(main):
                yield m
                if first <= i:
                    want = min(96, (i - first + 1) * 96 // (n1 - first - 12))
                    while gave < want:
                        yield ada[gave]
                        gave += 1

        FIRST = {"mkv", "mq", "mg", "dil", "gate", "ym", "diff", "yb", "ya", "wo"}
        stream = list(full_plan())
        for i in range(NRAW):
            sem(f"raw{i}")
        raw_free = [[] for _ in range(NRAW)]
        raw_cnt = [0] * NRAW
        spl_free = [[] for _ in range(NSPL)]
        state = {"piece": 0, "half": 0}
        halves = []
        adaq = []

        acc_blk = {}

        def fetch():
            i = state["piece"]
            state["piece"] += 1
            kind, key, segs = stream[i]
            r = i % NRAW
            rw = raw[:, r, :, :]
            for at, n, src in segs:
                if at == "dn":
                    dst = rw.rearrange("p (c a) n -> p c (a n)", a=2)
                else:
                    dst = rw[:, :, at:at + n]
                raw_cnt[r] += 16
                ld = sp.dma(dst, src, f"raw{r}", raw_cnt[r], raw_free[r])
            if kind == "w":
                toks = []
                for h in range(2):
                    s = state["half"] % NSPL
                    state["half"] += 1
                    src = rw[:, 2 * h:2 * h + 2, :]
                    th = sc.act(whi[:, s], src, ACT.Copy, ld, spl_free[s])
                    tl = ve.tt(wlo[:, s], src, whi[:, s].bitcast(F32), ALU.subtract, ld, th, spl_free[s])
                    toks.append(tl)
                    halves.append((key, s, [th, tl]))
                raw_free[r] = [toks[-1]]
            else:
                l, u, k = key
                if k == 0:
                    acc_blk[0] = mk_blk(2)
                b = acc_blk[0]
                t = None
                for c in range(4):
                    cc = c8[:, 4 * k + c:4 * k + c + 1]
                    if k == 0 and c == 0:
                        t = ve.ts(b.a, rw[:, c, :], cc, None, ALU.mult, None, ld, tc8, b.w)
                    else:
                        t = ve.stt(b.a, rw[:, c, :], cc, b.a, ALU.mult, ALU.add, ld, t or b.tok)
                    b.tok = [t]
                raw_free[r] = [t]
                if k == 1:
                    adaq.append((l, u, b))

        def ada_sums():
            while adaq:
                l, u, b = adaq.pop(0)
                g = gbank()
                for n in range(4):
                    t = pe.mm(GB[g][:, n:n + 1], b.a[:, n * P:n * P + P], ones[:, :], True, True,
                              gfree[g], b.tok, tconst, inc=(n == 3))
                b.release([t])
                m = l * 48 + u * 4
                tv = ve.tt(mod[:, m:m + 4], GB[g][:, 0:4], adb[:, m:m + 4], ALU.add, t, tadb)
                gfree[g] = [tv]
                mod_tok[l] = tv

        mod_tok = {}

        def take(key):
            while len(halves) < LOOK + 1 and state["piece"] < len(stream):
                fetch()
            k, s, t = halves.pop(0)
            assert k == key, (k, key)
            return s, t

        def gemm(A, b0, key, K, modes, evac):
            gs = [gbank(), gbank()]
            nk = K // P
            for kk in range(0, nk, 2):
                s, wt = take(key)
                pe.wait(wt, [t for b in range(b0 + kk, b0 + kk + 2) for t in A.tok[b]])
                if kk == 0:
                    pe.wait(gfree[gs[0]])
                    if modes != "TT":
                        pe.wait(gfree[gs[1]])
                todo = []
                for i in range(2):
                    kc, kb = kk + i, b0 + kk + i
                    fst, lst = kc == 0, kc == nk - 1
                    if modes == "TT":
                        for t in range(2):
                            o = GB[gs[t]][:, :]
                            a = (A.hi[:, kb, t * P:t * P + P], A.lo[:, kb, t * P:t * P + P])
                            w = (whi[:, s, i, :], wlo[:, s, i, :])
                            todo += [(t, o, a[0], w[0], fst, False), (t, o, a[0], w[1], False, False),
                                     (t, o, a[1], w[0], False, lst)]
                    else:
                        for hf in range(2):
                            for q in range(2):
                                o = GB[gs[hf]][:, q * 256:q * 256 + 256]
                                if modes[hf] == "F":
                                    c = hf * 256 + q * P
                                    a = (whi[:, s, i, c:c + P], wlo[:, s, i, c:c + P])
                                    w = (A.hi[:, kb, :], A.lo[:, kb, :])
                                else:
                                    a = (A.hi[:, kb, q * P:q * P + P], A.lo[:, kb, q * P:q * P + P])
                                    w = (whi[:, s, i, hf * 256:hf * 256 + 256],
                                         wlo[:, s, i, hf * 256:hf * 256 + 256])
                                f = fst and q == 0
                                todo += [(hf, o, a[0], w[0], f, False), (hf, o, a[0], w[1], False, False),
                                         (hf, o, a[1], w[0], False, lst)]
                if modes == "TT":
                    todo.sort(key=lambda z: z[0])
                second = False
                for n, (bk, o, a, w, f, e) in enumerate(todo):
                    if bk == 1 and not second and kk == 0:
                        pe.wait(gfree[gs[1]])
                        second = True
                    t = pe.mm(o, a, w, f, e, inc=(n == len(todo) - 1), skip=True)
                spl_free[s] = [t]
                if kk % 4 == 2:
                    if kk == nk - 2:
                        for b in range(b0, b0 + nk):
                            A.free[b] = [t]
                        for g in range(2):
                            gfree[gs[g]] = evac(g, GB[gs[g]], t)
                    ada_sums()
                    step()
            return t

        def load(eng, name, dst, src, *waits):
            sem(name)
            return eng.dma(dst, src, name, 16, *waits)

        vrows = mk_blk(1)
        vr = vrows.a[:, 0:P]
        tid = load(sp, "id", ident[:, :], C["ident"])
        sem("vr")
        tv0 = ve.memset(vr, 0.0)
        nv = 0

        def vload(dst, src, *w):
            nonlocal_n[0] += 16
            return sp.dma(dst, src, "vr", nonlocal_n[0], *w)

        nonlocal_n = [0]
        vload(vr[0:16, :], I["g_norm"].rearrange("l (a p) -> (l a) p", p=P), tv0)
        vload(vr[16:32, :], I["g_mem"].rearrange("l (a p) -> (l a) p", p=P))
        vload(vr[32:96, :], I["norm_gain_2"].rearrange("l j (a p) -> (l j a) p", p=P))
        vload(vr[96:104, :], I["c_2"].rearrange("l (a p) -> (l a) p", p=P))
        vload(vr[104:106, :], I["gla_head_norm_2"].rearrange("l (a p) -> (l a) p", p=P))
        vload(vr[106:114, :], I["g_final"].rearrange("(a p) -> a p", p=P))
        tvr = vload(vr[114:122, :], I["final_norm_2"].rearrange("(a p) -> a p", p=P))
        COL = dict(g_norm=0, g_mem=16, gain=32, c=96, head=104, g_final=106, f_norm=114)
        ab = [mk_blk(1), mk_blk(1)]
        abv = I["ada_b_2"].rearrange("l (a p) -> (l a) p", p=P)
        tab = [load(sp, f"ab{i}", ab[i].a[0:96, 0:P], abv[96 * i:96 * i + 96, :]) for i in range(2)]
        tx = load(sp, "x", X[:, :, :], I["x"][0].rearrange("(t p) d -> p t d", p=P))
        memb = mk_blk(8)
        tmem = load(sp, "mem0", memb.a.rearrange("p (t d) -> p t d", t=2),
                    I["mem"][0].rearrange("(t p) d -> p t d", p=P), memb.w)
        lamb = mk_blk(2)
        tlam = load(po, "lam", lamb.a, I["diff_lambda"].rearrange("l a b -> (l a b)").unsqueeze(0).to_broadcast([P, 512]))
        ohb = mk_blk(4)
        oh, dmk, rbt = ohb.a[0:32, 0:512], ohb.a[0:20, 512:1024], None
        rbb = mk_blk(3)
        rbt = rbb.a[0:32, 0:20]
        toh = load(po, "oh", oh, C["onehot"])
        tdm = load(po, "dm", dmk, C["dilmask"])
        trb = load(po, "rb", rbt, I["rel_bias"])
        t1 = ve.memset(ones[:, :], 1.0)
        t2 = ve.memset(mhalf[:, :], -0.5)
        tconst = [t1, t2]

        g = gbank()
        t = pe.tr(GB[g][:, 0:P], vr, ident[:, :], tid, tvr, tv0, inc=True)
        tcols = ve.copy(cols[:, :], GB[g][:, 0:P], t)
        gfree[g] = [tcols]
        vrows.release([t])
        g = gbank()
        for i in range(2):
            t = pe.tr(GB[g][:, 96 * i:96 * i + 96], ab[i].a[0:96, 0:P], ident[0:96, 0:96], tab[i], inc=True)
            ab[i].release([t])
        tadb = ve.copy(adb[:, :], GB[g][:, 0:192], t)
        gfree[g] = [tadb]
        ccol = cols[:, COL["c"]:COL["c"] + 8]
        th = smc(8)
        t = sc.act(th, ccol, ACT.Tanh, tcols, scale=0.5)
        t = ve.stt(th, th, 1.0, ccol, ALU.add, ALU.mult, t)
        tc8 = ve.ts(c8[:, :], th, 0.5, None, ALU.mult, None, t)

        lm = smc(4)
        lprod = lamb.a.rearrange("p (l a b) -> p l a b", l=2, a=4)
        pr = rbb.a[:, 64:320].rearrange("p (l c b) -> p l c b", l=2, c=2)
        t = ve.tt(pr, lprod[:, :, 0::2, :], lprod[:, :, 1::2, :], ALU.mult, tlam)
        t = ve.red(lm, pr.rearrange("p l c b -> p (l c) b"), ALU.add, t)
        t = sc.act(lm, lm, ACT.Exp, t)
        lm2 = lm.rearrange("p (l c) -> p l c", c=2)
        t = ve.tt(nlam[:, :], lm2[:, :, 1], lm2[:, :, 0], ALU.subtract, t)
        lam_init = [0.8 - 0.6 * math.exp(-0.3 * l) for l in range(2)]
        for l in range(2):
            tnlam = ve.ts(nlam[:, l:l + 1], nlam[:, l:l + 1], -lam_init[l], None, ALU.add, None, t)
        lamb.release([t])

        g = gbank()
        t = pe.mm(GB[g][0:20, :], rbt, oh, True, True, toh, trb, inc=True)
        btb = mk_blk(2)
        t2 = ve.tt(btb.a[0:20, :], GB[g][0:20, :], dmk, ALU.add, t, tdm)
        gfree[g] = [t2]
        tscr = load(po, "scr", scratch, btb.a[0:20, :].unsqueeze(1).to_broadcast([20, P, 512]), t2)
        for b in (ohb, rbb):
            b.release([t2, t, tnlam])
        btb.release([tscr])

        for i in range(6):
            sem(f"bias{i}")
        bias_free = [[] for _ in range(6)]
        bias_c = [0] * 6

        def get_bias(sl, i, h):
            r = 3 * sl.j + i
            bias_c[r] += 16
            src = bass.AP(scratch.tensor, h * P * 512 + 127, [[511, P], [1, 384]])
            t = po.dma(bias_t[:, r, :], src, f"bias{r}", bias_c[r], tscr, bias_free[r])
            return r, t

        def rstd_of(ss, n, mult, *w):
            ms = smc(n)
            t = ve.ts(ms, ss, mult, EPS, ALU.mult, ALU.add, *w)
            r = smc(n)
            t = po.tt(r, ms, mhalf[:, 0:n], ALU.pow, t, tconst)
            return r, t

        def normed(src, stok):
            nb = mk_blk(8)
            xn = nb.a.rearrange("p (t d) -> p t d", t=2)
            ss = smc(2)
            ts_ = [sc.act(xn[:, t, :], src[:, t, :], ACT.Square, stok, nb.w, accum=ss[:, t:t + 1])
                   for t in range(2)]
            r, tr_ = rstd_of(ss, 2, 1.0 / D, *ts_)
            ta = ve.ts(xn[:, 0, :], src[:, 0, :], r[:, 0:1], None, ALU.mult, None, tr_)
            tb = sc.act(xn[:, 1, :], src[:, 1, :], ACT.Copy, tr_, scale=r[:, 1:2])
            nb.tok = [ta, tb]
            return nb, xn

        def to_T(src, stok, dst, scol=None, bcol=None, const=1.0, ctok=None, nk=8, hn=False):
            done = []
            for b in range(nk // 2):
                g = gbank()
                for i in range(2):
                    for t in range(2):
                        kc = 2 * b + i
                        tk = pe.tr(GB[g][:, i * 256 + t * P:i * 256 + t * P + P],
                                   src[:, t, kc * P:kc * P + P], ident[:, :], stok, gfree[g], tid,
                                   inc=(i == 1 and t == 1))
                hi = dst.hi[:, 2 * b:2 * b + 2, :].rearrange("p a c -> p (a c)")
                lo = dst.lo[:, 2 * b:2 * b + 2, :].rearrange("p a c -> p (a c)")
                fr = dst.waits(2 * b, 2)
                if scol is None:
                    t1 = sc.act(hi, GB[g][:, :], ACT.Copy, tk, fr, scale=const)
                    t2 = ve.stt(lo, GB[g][:, :], const, hi.bitcast(F32), ALU.mult, ALU.subtract, t1, fr)
                    gfree[g] = [t2]
                else:
                    tmp = mk_blk(2)
                    for i in range(2):
                        kc = (2 * b + i) % 2 if hn else 2 * b + i
                        s1 = scol[:, kc:kc + 1]
                        ps = GB[g][:, i * 256:i * 256 + 256]
                        o = tmp.a[:, i * 256:i * 256 + 256]
                        if bcol is None:
                            tv = ve.ts(o, ps, s1, None, ALU.mult, None, tk, ctok, tmp.w)
                        else:
                            tv = ve.ts(o, ps, s1, bcol[:, kc:kc + 1], ALU.mult, ALU.add, tk, ctok, tmp.w)
                    gfree[g] = [tv]
                    t1 = sc.act(hi, tmp.a, ACT.Copy, tv, fr)
                    t2 = ve.tt(lo, tmp.a, hi.bitcast(F32), ALU.subtract, t1, tv, fr)
                    tmp.release([t2])
                dst.write(2 * b, 2, [t1, t2])
                done = [tk]
            return done

        def split_ps(dst_hi, dst_lo, src, fr, *w):
            t1 = sc.act(dst_hi, src, ACT.Copy, fr, *w)
            t2 = ve.tt(dst_lo, src, dst_hi.bitcast(F32), ALU.subtract, fr, t1, *w)
            return [t1, t2]

        def exps(S, ap_list, nm, sums, *w):
            for n, a in enumerate(ap_list):
                t = sc.act(a, a, ACT.Exp, *w, bias=nm[:, n:n + 1], accum=sums[:, n:n + 1])
            return t

        def diff_head(l, h, qb, kb, vb, hs):
            def task(sl):
                j = h % 4
                q = qb.a.rearrange("p (m b c) -> p m b c", m=2, b=2)
                k = kb.a.rearrange("p (m b c) -> p m b c", m=2, b=2)
                p0 = 64 * (j % 2)
                vv = vb.a.rearrange("p (t e) -> p t e", t=2)[:, :, j * P:j * P + P]
                r, tb = get_bias(sl, 0, h)
                yield
                for t in range(2):
                    for m in range(2):
                        tk = pe.mm(sl.ps[:, t, m * 256:m * 256 + 256], q[p0:p0 + 64, m, j // 2, t * P:t * P + P],
                                   k[p0:p0 + 64, m, j // 2, :], True, True, qb.tok, kb.tok, sl.ps_free,
                                   inc=(t == 1 and m == 1))
                yield
                S = sl.S[:, 0:1024].rearrange("p (t m k) -> p t m k", t=2, m=2)
                for t in range(2):
                    bt = bias_t[:, r, 128 - 128 * t:384 - 128 * t].unsqueeze(1).to_broadcast([P, 2, 256])
                    tv = ve.stt(S[:, t], sl.ps[:, t, :].rearrange("p (m k) -> p m k", m=2), 0.125, bt,
                                ALU.mult, ALU.add, tk, tb, sl.S_free)
                bias_free[r] = [tv]
                nm, su = smc(4), smc(4)
                S4 = sl.S[:, 0:1024].rearrange("p (n k) -> p n k", n=4)
                tn = ve.red(nm, S4, ALU.max, tv, negate=True)
                te = exps(S4, [S4[:, n, :] for n in range(4)], nm, su, tn, tv)
                yield
                rc = smc(4)
                t1 = ve.recip(rc, su, te)
                r1 = smc(2)
                rc2 = rc.rearrange("p (t m) -> p t m", m=2)
                t1 = ve.ts(r1, rc2[:, :, 1], nlam[:, l:l + 1], None, ALU.mult, None, t1, tnlam)
                for t in range(2):
                    ta = ve.ts(S[:, t, 1, :], S[:, t, 1, :], r1[:, t:t + 1], None, ALU.mult, None, t1, te)
                    ta = ve.stt(S[:, t, 0, :], S[:, t, 0, :], rc[:, 2 * t:2 * t + 1], S[:, t, 1, :],
                                ALU.mult, ALU.add, ta)
                yield
                for kc in range(2):
                    for t in range(2):
                        tk = pe.tr(sl.ps[:, 0, kc * 256 + t * P:kc * 256 + t * P + P],
                                   S[:, t, 0, kc * P:kc * P + P], ident[:, :], ta, inc=(kc == 1 and t == 1))
                sl.S_free = [tk]
                yield
                tw = sc.act(sl.W[:, 0:512], sl.ps[:, 0, :], ACT.Copy, tk, sl.W_free)
                yield
                for t in range(2):
                    for kc in range(2):
                        tk = pe.mm(sl.ps[:, 1, t * P:t * P + P], sl.W[:, kc * 256 + t * P:kc * 256 + t * P + P],
                                   vv[:, kc, :], kc == 0, kc == 1, tw, vb.tok, inc=(kc == 1 and t == 1))
                sl.W_free = [tk]
                yield
                ss = smc(2)
                for t in range(2):
                    t1 = sc.act(sl.W[:, 1024 + t * P:1024 + t * P + P], sl.ps[:, 1, t * P:t * P + P], ACT.Square,
                                tk, accum=ss[:, t:t + 1])
                t2 = ve.copy(vv, sl.ps[:, 1, 0:256].rearrange("p (t e) -> p t e", t=2), tk, t1)
                sl.ps_free = [t2]
                sl.W_free = sl.W_free + [t1]
                rs, tr_ = rstd_of(ss, 2, 1.0 / P, t1)
                yield
                rs2 = smc(2)
                t3 = ve.ts(rs2, rs, 0.5 * (1.0 - lam_init[l]), None, ALU.mult, None, tr_)
                gg = hs["g"].a.rearrange("p (t e) -> p t e", t=2)[:, :, j * P:j * P + P]
                for t in range(2):
                    t4 = ve.stt(vv[:, t, :], vv[:, t, :], rs2[:, t:t + 1], gg[:, t, :], ALU.mult, ALU.mult,
                                t2, t3, hs["g"].tok)
                hs["out"].append(t4)
                hs["n"] += 1
                if j == 3:
                    pass
                if hs["n"] == 4:
                    qb.release([t4])
                    kb.release([t4])
            return task

        def dil_head(l, hh, blk, st):
            def task(sl):
                j = hh % 2
                bs = [get_bias(sl, gi, 8 + gi * 4 + hh) for gi in range(3)]
                yield
                for t in range(2):
                    for gi in range(3):
                        o = sl.ps[:, gi // 2, (gi % 2) * 256:(gi % 2) * 256 + 256]
                        tk = pe.mm(o, blk["q"](gi, j)[:, t * P:t * P + P], blk["k"](gi, j), True, True,
                                   blk["qk_tok"](), sl.ps_free, inc=(gi == 2))
                    yield
                    S = sl.S[:, 0:768].rearrange("p (g k) -> p g k", g=3)
                    psf = sl.ps[:, :, :].rearrange("p a b -> p (a b)")
                    for gi in range(3):
                        r, tb = bs[gi]
                        tv = ve.stt(S[:, gi, :], psf[:, gi * 256:gi * 256 + 256], 128 ** -0.5,
                                    bias_t[:, r, 128 - 128 * t:384 - 128 * t], ALU.mult, ALU.add, tk, tb, sl.S_free)
                        if t == 1:
                            bias_free[r] = [tv]
                    nm, su = smc(1), smc(1)
                    tn = ve.red(nm, sl.S[:, 0:768], ALU.max, tv, negate=True)
                    te = sc.act(sl.S[:, 0:768], sl.S[:, 0:768], ACT.Exp, tn, tv, bias=nm, accum=su)
                    yield
                    rc = smc(1)
                    t1 = ve.recip(rc, su, te)
                    t1 = ve.ts(sl.S[:, 0:768], sl.S[:, 0:768], rc, 0.5, ALU.mult, ALU.mult, t1, te)
                    yield
                    for n in range(6):
                        tk = pe.tr(psf[:, n * P:n * P + P], sl.S[:, n * P:n * P + P], ident[:, :], t1, tv,
                                   inc=(n == 5))
                    sl.S_free = [tk]
                    yield
                    W = sl.W[:, :].rearrange("p (n q) -> p n q", n=6)
                    tw = sc.act(W[:, :, t * P:t * P + P], psf[:, 0:768].rearrange("p (n q) -> p n q", n=6),
                                ACT.Copy, tk, sl.W_free)
                    sl.ps_free = [tw]
                for n in range(6):
                    tk = pe.mm(sl.ps[:, 0, 0:256], blk["v"](n // 2, n % 2, j), W[:, n, :], n == 0, n == 5,
                               tw, blk["v_tok"](), inc=(n == 5))
                sl.W_free = [tk]
                yield
                tmp = Blk(1)
                t1 = ve.tt(tmp.a, sl.ps[:, 0, 0:256], blk["g"](j), ALU.mult, tk, blk["g_tok"](), tmp.w)
                sl.ps_free = [t1]
                b = 4 + hh
                OT.write(b, 1, split_ps(OT.hi[:, b, :], OT.lo[:, b, :], tmp.a, OT.waits(b, 1), t1))
                tmp.release(OT.tok[b])
                st["n"] += 1
                if st["n"] == 2:
                    for bb in blk["all"]:
                        bb.release([t1, tk])
            return task

        def mem_head(l, h, B, st):
            def task(sl):
                yield
                q, k, v, gt = B["q"], B["k"], B["v"], B["g"]
                for t in range(2):
                    tk = pe.mm(sl.ps[:, 0, t * 256:t * 256 + 256], q.a[:, h * 256 + t * P:h * 256 + t * P + P],
                               k.a[:, h * 256:h * 256 + 256], True, True, q.tok, k.tok, sl.ps_free, inc=(t == 1))
                yield
                nm, su = smc(2), smc(2)
                p2 = sl.ps[:, 0, :].rearrange("p (t k) -> p t k", t=2)
                S = sl.S[:, 0:512].rearrange("p (t k) -> p t k", t=2)
                tn = ve.red(nm, p2, ALU.max, tk, negate=True)
                nm2 = smc(2)
                tn = ve.ts(nm2, nm, 128 ** -0.5, None, ALU.mult, None, tn)
                for t in range(2):
                    te = sc.act(S[:, t, :], p2[:, t, :], ACT.Exp, tn, sl.S_free, bias=nm2[:, t:t + 1],
                                scale=128 ** -0.5, accum=su[:, t:t + 1])
                yield
                rc = smc(2)
                t1 = ve.recip(rc, su, te)
                for t in range(2):
                    t2 = ve.ts(S[:, t, :], S[:, t, :], rc[:, t:t + 1], 0.5, ALU.mult, ALU.mult, t1, te)
                yield
                for kc in range(2):
                    for t in range(2):
                        tk = pe.tr(sl.ps[:, 1, kc * 256 + t * P:kc * 256 + t * P + P],
                                   S[:, t, kc * P:kc * P + P], ident[:, :], t2, inc=(kc == 1 and t == 1))
                sl.S_free = [tk]
                yield
                tw = sc.act(sl.W[:, 0:512], sl.ps[:, 1, :], ACT.Copy, tk, sl.W_free)
                yield
                for kc in range(2):
                    tk = pe.mm(sl.ps[:, 0, 0:256], v.a[:, kc * 512 + h * P:kc * 512 + h * P + P],
                               sl.W[:, kc * 256:kc * 256 + 256], kc == 0, kc == 1, tw, v.tok, inc=(kc == 1))
                sl.W_free = [tk]
                yield
                tmp = Blk(1)
                t1 = ve.tt(tmp.a, sl.ps[:, 0, 0:256], gt.a[:, h * 256:h * 256 + 256], ALU.mult, tk, gt.tok, tmp.w)
                sl.ps_free = [t1]
                OT.write(h, 1, split_ps(OT.hi[:, h, :], OT.lo[:, h, :], tmp.a, OT.waits(h, 1), t1))
                tmp.release(OT.tok[h])
                st["n"] += 1
                if st["n"] == 4:
                    for bb in (q, k, v, gt):
                        bb.release([t1, tk])
            return task

        def ev_copy(blk, view):
            def f(g, ps, t):
                tc = sc.act(view(g), ps[:, :], ACT.Copy, t, blk.w)
                blk.tok = blk.tok + [tc]
                return [tc]
            return f

        def quad(b, g):
            return b.a[:, g * 512:g * 512 + 512]

        def silu2(dst, ps, t, blk):
            t1 = sc.act(dst, ps, ACT.Tanh, t, blk.w, scale=0.5)
            t2 = ve.stt(dst, dst, 1.0, ps, ALU.add, ALU.mult, t1)
            blk.tok = blk.tok + [t2]
            return [t2]

        xtok = [tx]

        def layer1(l):
            nonlocal_x = xtok
            if l == 0:
                mb, tm = memb, tmem
            else:
                mb = mk_blk(8)
                tm = load(po, "mem1", mb.a.rearrange("p (t d) -> p t d", t=2),
                          I["mem"][0].rearrange("(t p) d -> p t d", p=P), mb.w)
            nb, mn = normed(mb.a.rearrange("p (t d) -> p t d", t=2), [tm])
            mb.release(nb.tok)
            gm = cols[:, COL["g_mem"] + 8 * l:COL["g_mem"] + 8 * l + 8]
            rel = to_T(mn, nb.tok, OT, scol=gm, ctok=tcols)
            nb.release(rel)
            B = {"k": mk_blk(4), "v": mk_blk(4)}
            gemm(OT, 0, ("mkv", l, 0), D, "FF", ev_copy(B["k"], lambda g: quad(B["k"], g)))
            nb, xn = normed(X, nonlocal_x)
            gemm(OT, 0, ("mkv", l, 1), D, "TT", ev_copy(B["v"], lambda g: quad(B["v"], g)))
            gn = cols[:, COL["g_norm"] + 8 * l:COL["g_norm"] + 8 * l + 8]
            rel = to_T(xn, nb.tok, HT, scol=gn, ctok=tcols)
            nb.release(rel)
            B["q"], B["g"] = mk_blk(4), mk_blk(4)
            gemm(HT, 0, ("mq", l), D, "FF", ev_copy(B["q"], lambda g: quad(B["q"], g)))
            gemm(HT, 0, ("mg", l), D, "FF", lambda g, ps, t: silu2(quad(B["g"], g), ps[:, :], t, B["g"]))
            st = {"n": 0}
            for h in range(4):
                pend.append(mem_head(l, h, B, st))
            sts = [st]
            for pr in range(2):
                b1, b2, b3, b4, b5 = mk_blk(4), mk_blk(4), mk_blk(4), mk_blk(4), mk_blk(4)
                gemm(HT, 0, ("dil", l, pr, 0), D, "FF", ev_copy(b1, lambda g: quad(b1, g)))
                gemm(HT, 0, ("dil", l, pr, 1), D, "FF", ev_copy(b2, lambda g: quad(b2, g)))
                gemm(HT, 0, ("dil", l, pr, 2), D, "FF", ev_copy(b3, lambda g: quad(b3, g)))
                gemm(HT, 0, ("dil", l, pr, 3), D, "TT", ev_copy(b4, lambda g: quad(b4, g)))

                def ev(g, ps, t, b5=b5):
                    if g == 0:
                        tc = sc.act(quad(b5, 0), ps[:, :], ACT.Copy, t, b5.w)
                        b5.tok = b5.tok + [tc]
                        return [tc]
                    return silu2(quad(b5, 1), ps[:, :], t, b5)
                gemm(HT, 0, ("dil", l, pr, 4), D, "TF", ev)

                def bl(b, n):
                    return b.a[:, n * 256:n * 256 + 256]

                def vv(gi, kc, j, b4=b4, b5=b5):
                    if gi < 2:
                        return b4.a[:, kc * 512 + gi * 256 + j * P:kc * 512 + gi * 256 + j * P + P]
                    return b5.a[:, kc * 256 + j * P:kc * 256 + j * P + P]
                blk = {"q": lambda gi, j, b1=b1, b2=b2: bl(b1, gi * 2 + j) if gi < 2 else bl(b2, j),
                       "k": lambda gi, j, b2=b2, b3=b3: bl(b3, gi * 2 + j) if gi < 2 else bl(b2, 2 + j),
                       "v": vv, "g": lambda j, b5=b5: bl(b5, 2 + j),
                       "qk_tok": lambda b1=b1, b2=b2, b3=b3: b1.tok + b2.tok + b3.tok,
                       "v_tok": lambda b4=b4, b5=b5: b4.tok + b5.tok, "g_tok": lambda b5=b5: b5.tok,
                       "all": [b1, b2, b3, b4, b5]}
                st2 = {"n": 0}
                sts.append(st2)
                for hh in (2 * pr, 2 * pr + 1):
                    pend.append(dil_head(l, hh, blk, st2))
            merged = mk_blk(8)
            mg = merged.a.rearrange("p (t d) -> p t d", t=2)
            mtok = {}

            def gate_of(i, u):
                gb = mk_blk(4)

                def ev(g, ps, t):
                    tc = sc.act(quad(gb, g), ps[:, :], ACT.Tanh, t, gb.w, scale=0.5)
                    gb.tok = gb.tok + [tc]
                    return [tc]
                gemm(HT, 0, ("gate", l, i, u), D, "TT", ev)
                return gb

            def y_of(key, A, b0, K, u, gb, first):
                last = []

                def ev(g, ps, t):
                    m = mg[:, g, u * 512:u * 512 + 512]
                    if first:
                        tv = ve.stt(m, quad(gb, g), 1.0, ps[:, :], ALU.add, ALU.mult, t, gb.tok, merged.w)
                        mtok[(g, u)] = tv
                    else:
                        tv = ve.stt(quad(gb, g), quad(gb, g), 1.0, ps[:, :], ALU.add, ALU.mult, t, gb.tok)
                        mtok[(g, u)] = po.tt(m, m, quad(gb, g), ALU.add, tv, mtok[(g, u)])
                    last.append(tv)
                    last.append(mtok[(g, u)])
                    return [tv]
                gemm(A, b0, key, K, "TT", ev)
                gb.release(last)

            for u in range(2):
                gb = gate_of(2, u)
                drain(lambda: sts[0]["n"] == 4)
                y_of(("ym", l, u), OT, 0, 512, u, gb, True)
            V = []
            for hf in range(2):
                qb, kb, vb, gb = mk_blk(4), mk_blk(4), mk_blk(4), mk_blk(4)
                gemm(HT, 0, ("diff", l, hf, 0), D, "FF", ev_copy(qb, lambda g: quad(qb, g)))
                gemm(HT, 0, ("diff", l, hf, 1), D, "FF", ev_copy(kb, lambda g: quad(kb, g)))
                gemm(HT, 0, ("diff", l, hf, 2), D, "TT", ev_copy(vb, lambda g: quad(vb, g)))
                hs = {"g": gb, "out": [], "n": 0}
                gemm(HT, 0, ("diff", l, hf, 3), D, "TT",
                     lambda g, ps, t, gb=gb: silu2(quad(gb, g), ps[:, :], t, gb))
                for h in range(4 * hf, 4 * hf + 4):
                    pend.append(diff_head(l, h, qb, kb, vb, hs))
                V.append((vb, gb, hs))
            drain(lambda: all(s["n"] == 2 for s in sts[1:]))
            for u in range(2):
                gb = gate_of(1, u)
                y_of(("yb", l, u), OT, 4, 512, u, gb, False)
            gbs = [gate_of(0, u) for u in range(2)]
            drain(lambda: not busy())
            for hf in range(2):
                vb, gb, hs = V[hf]
                src = vb.a.rearrange("p (t e) -> p t e", t=2)
                sub = Sub(OT, 4 * hf)
                rel = to_T(src, hs["out"], sub, nk=4)
                vb.release(rel)
                gb.release(hs["out"])
            for u in range(2):
                y_of(("ya", l, u), OT, 0, D, u, gbs[u], False)
            rel = to_T(mg, list(mtok.values()), HT, const=0.5)
            merged.release(rel)
            nx = []
            for u in range(2):
                def ev(g, ps, t):
                    xs = X[:, g, u * 512:u * 512 + 512]
                    tv = ve.tt(xs, ps[:, :], xs, ALU.add, t, xtok)
                    nx.append(tv)
                    return [tv]
                gemm(HT, 0, ("wo", l, u), D, "TT", ev)
            xtok[:] = nx

        class Sub:

            def __init__(self, A, b0):
                self.A, self.b0 = A, b0
                self.hi, self.lo = A.hi[:, b0:8, :], A.lo[:, b0:8, :]

            def write(self, b, n, t):
                self.A.write(self.b0 + b, n, t)

            def waits(self, b, n):
                return self.A.waits(self.b0 + b, n)

        def bcast(c0, src, stok):
            b = mk_blk(4)
            for hf in range(2):
                g = gbank()
                for n in range(4):
                    c = c0 + hf * 4 + n
                    t = pe.mm(GB[g][:, n * P:n * P + P], src[:, c:c + 1].to_broadcast([P, P]), ident[:, :], True, True,
                              stok, gfree[g], inc=(n == 3))
                tv = sc.act(b.a[:, hf * 512:hf * 512 + 512], GB[g][:, :], ACT.Copy, t, b.w)
                gfree[g] = [tv]
                b.tok = b.tok + [tv]
            return b

        def final_norm(c0, dst):
            gb = bcast(c0, cols, tcols)
            nb, xn = normed(X, xtok)
            ts_ = [ve.tt(dst[:, t, :], xn[:, t, :], gb.a, ALU.mult, nb.tok, gb.tok) for t in range(2)]
            nb.release(ts_)
            gb.release(ts_)
            return ts_

        def modulated(l, jn):
            m = mod[:, l * 48 + jn * 24:l * 48 + jn * 24 + 24]
            gain = cols[:, COL["gain"] + 16 * l + 8 * jn:COL["gain"] + 16 * l + 8 * jn + 8]
            a = smc(8)
            ta = ve.stt(a, m[:, 8:16], 1.0, gain, ALU.add, ALU.mult, mod_tok[l], tcols)
            nb, xn = normed(X, xtok)
            rel = to_T(xn, nb.tok, HT, scol=a, bcol=m[:, 0:8], ctok=[ta, mod_tok[l]])
            nb.release(rel)

        def residual(gb, u, nx):
            def ev(g, ps, t):
                tmp = mk_blk(2)
                xs = X[:, g, u * 512:u * 512 + 512]
                t1 = ve.tt(tmp.a, ps[:, :], gb.a[:, u * 512:u * 512 + 512], ALU.mult, t, gb.tok, tmp.w)
                t2 = po.tt(xs, xs, tmp.a, ALU.add, t1, xtok)
                tmp.release([t2])
                nx.append(t2)
                return [t1]
            return ev

        def softmax_pv4(sl, t, nk, S3, wd, tv, tn, nm, v_of, vtok, ob, extra=0):
            su = smc(4)
            te = exps(None, [S3[:, n, 0:wd] for n in range(4)], nm, su, tn, tv)
            yield
            rc = smc(4)
            t1 = ve.recip(rc, su, te)
            K = nk * P
            for n in range(4):
                t2 = ve.ts(S3[:, n, 0:K], S3[:, n, 0:K], rc[:, n:n + 1], None, ALU.mult, None, t1, te)
            yield
            psf = sl.ps[:, :, :].rearrange("p a b -> p (a b)")
            for kc in range(nk):
                for n in range(4):
                    tk = pe.tr(psf[:, (kc * 4 + n) * P:(kc * 4 + n) * P + P], S3[:, n, kc * P:kc * P + P],
                               ident[:, :], t2, inc=(kc == nk - 1 and n == 3))
            sl.S_free = [tk]
            yield
            tw = []
            for kc in range(nk):
                eng = sc if kc == 0 else ve
                o, i = sl.W[:, kc * 512:kc * 512 + 512], sl.ps[:, kc, :]
                tw.append(sc.act(o, i, ACT.Copy, tk, sl.W_free) if kc == 0 else ve.copy(o, i, tk, sl.W_free))
            yield
            W = sl.W[:, 0:1024].rearrange("p (k n q) -> p k n q", k=2, n=4)
            for hp in range(2):
                for kc in range(nk):
                    o = sl.ps[64 * hp:64 * hp + 64, 0, 0:256].rearrange("p (n q) -> p n q", n=2)
                    tk = pe.mm(o, v_of(kc, hp), W[:, kc, 2 * hp:2 * hp + 2, :], kc == 0, kc == nk - 1, tw, vtok,
                               inc=(hp == 1 and kc == nk - 1), skip=True)
            sl.W_free = [tk]
            yield
            o = sl.ps[:, 0, 0:256].rearrange("p (n q) -> p n q", n=2)
            tt_ = split_ps(OT.hi[:, ob:ob + 2, t * P:t * P + P], OT.lo[:, ob:ob + 2, t * P:t * P + P], o,
                           OT.waits(ob, 2), tk)
            for b in (ob, ob + 1):
                OT.tok[b] = OT.tok[b] + tt_
            sl.ps_free = [tt_[-1]]

        def swa_layer(l):
            j = l // 3
            gb = bcast(l * 48 + 16, mod, mod_tok[l])
            cb = mk_blk(3)
            rp = cb.a[:, 0:256].rearrange("p (s t d) -> p s t d", s=2, t=2)
            msk = cb.a[:, 256:512]
            snk = cb.a[:, 512:528]
            trp = load(po, f"rp{l}", cb.a[:, 0:256], C["rope"], cb.w)
            tms = load(po, f"ms{l}", msk, C["swamask"], cb.w)
            tsk = load(po, f"sk{l}", snk, I["swa_sinks_2"][j].unsqueeze(0).to_broadcast([P, 16]), cb.w)
            modulated(l, 0)

            def rope_bank(ps, t, dst, nh, tb, blk):
                tmp = Blk(2)
                x = ps[:, 0:nh * 64].rearrange("p (h a b) -> p h a b", a=2, b=32)
                d = dst[:, 0:nh * 64].rearrange("p (h a b) -> p h a b", a=2, b=32)
                m = tmp.a[:, 0:nh * 64].rearrange("p (h a b) -> p h a b", a=2, b=32)
                c = rp[:, 0, t, :].rearrange("p (a b) -> p a b", a=2).unsqueeze(1).to_broadcast([P, nh, 2, 32])
                s = rp[:, 1, t, :].rearrange("p (a b) -> p a b", a=2).unsqueeze(1).to_broadcast([P, nh, 2, 32])
                t1 = ve.tt(d, x, c, ALU.mult, tb, trp, blk.w)
                t2 = ve.tt(m, x[:, :, ::-1, :], s, ALU.mult, tb, trp, tmp.w)
                t3 = po.tt(dst[:, 0:nh * 64], dst[:, 0:nh * 64], tmp.a[:, 0:nh * 64], ALU.add, t1, t2)
                tmp.release([t3])
                return t2, t3

            kvb = mk_blk(4)

            def ev_kv(g, ps, t):
                t2, t3 = rope_bank(ps, g, kvb.a[:, g * 512:g * 512 + 256], 4, t, kvb)
                t4 = sc.act(kvb.a[:, g * 512 + 256:g * 512 + 512], ps[:, 256:512], ACT.Copy, t, t2, kvb.w)
                kvb.tok = kvb.tok + [t3, t4]
                return [t4]
            gemm(HT, 0, ("swa", l, 2), D, "TT", ev_kv)
            kT = mk_blk(4)
            kt = kT.a.rearrange("p (n c) -> p n c", n=4)
            for n2 in range(2):
                g = gbank()
                for n in (2 * n2, 2 * n2 + 1):
                    for t in range(2):
                        for dup in range(2):
                            c = (n % 2) * 256 + t * P
                            tk = pe.mm(GB[g][64 * dup:64 * dup + 64, c:c + P],
                                       kvb.a[:, t * 512 + n * 64:t * 512 + n * 64 + 64], ident[:, :], True, True,
                                       kvb.tok, gfree[g], inc=(n % 2 == 1 and t == 1 and dup == 1), skip=True)
                tc = sc.act(kT.a[:, n2 * 512:n2 * 512 + 512], GB[g][:, :], ACT.Copy, tk, kT.w)
                gfree[g] = [tc]
                kT.tok = kT.tok + [tc]
            st = {"n": 0, "t": []}
            qTs = []
            for b in range(8):
                OT.tok[b] = []

            def head4(kv, t, qT):
                def task(sl):
                    q = qT.a.rearrange("p (n c) -> p n c", n=4)
                    nk, k0 = t + 1, 0
                    K = nk * P
                    wd = K + 1
                    yield
                    for n in range(4):
                        h = 4 * kv + ORD[n]
                        p0 = 64 * (h % 2)
                        tk = pe.mm(sl.ps[:, n // 2, (n % 2) * 256:(n % 2) * 256 + K],
                                   q[p0:p0 + 64, (h // 2) % 4, t * P:t * P + P], kt[p0:p0 + 64, kv, 0:K], True, True,
                                   qT.tok, kT.tok, sl.ps_free, inc=(n == 3))
                    yield
                    S3 = sl.S[:, 0:4 * 257].rearrange("p (n k) -> p n k", n=4)
                    p4 = sl.ps[:, :, :].rearrange("p a (b k) -> p (a b) k", b=2)[:, :, 0:K]
                    mk = msk[:, 256 - K:256].unsqueeze(1).to_broadcast([P, 4, K])
                    t1 = ve.stt(S3[:, :, 0:K], p4, 0.125, mk, ALU.mult, ALU.add, tk, tms, sl.S_free)
                    t2 = ve.copy(S3[:, :, K].rearrange("p (a b) -> p a b", a=2),
                                 snk[:, 4 * kv:4 * kv + 4].rearrange("p (b a) -> p a b", a=2), tsk, sl.S_free)
                    nm = smc(4)
                    tn = ve.red(nm, S3[:, :, 0:wd], ALU.max, t1, t2, negate=True)

                    def v_of(kc, hp):
                        return kvb.a[:, kc * 512 + 256 + kv * 64:kc * 512 + 256 + kv * 64 + 64]
                    yield from softmax_pv4(sl, t, nk, S3, wd, t1, tn, nm, v_of, kvb.tok, 2 * kv)
                    st["n"] += 1
                    st["t"] += [sl.ps_free[0]]
                return task

            for u in range(2):
                qt = mk_blk(4)

                def ev_q(g, ps, t):
                    t2, t3 = rope_bank(ps, g, qt.a[:, g * 512:g * 512 + 512], 8, t, qt)
                    qt.tok = qt.tok + [t3]
                    return [t2]
                gemm(HT, 0, ("swa", l, u), D, "TT", ev_q)
                qT = mk_blk(4)
                for n2 in range(2):
                    g = gbank()
                    for n in range(2):
                        for t in range(2):
                            c = t * 512 + (n2 * 2 + n) * P
                            tk = pe.tr(GB[g][:, n * 256 + t * P:n * 256 + t * P + P], qt.a[:, c:c + P], ident[:, :],
                                       qt.tok, gfree[g], inc=(n == 1 and t == 1))
                    tc = sc.act(qT.a[:, n2 * 512:n2 * 512 + 512], GB[g][:, :], ACT.Copy, tk, qT.w)
                    gfree[g] = [tc]
                    qT.tok = qT.tok + [tc]
                qt.release([tk])
                qTs.append(qT)
                for kv in (2 * u, 2 * u + 1):
                    for t in range(2):
                        pend.append(head4(kv, t, qT))
            drain(lambda: not busy())
            for b in qTs + [kT, kvb, cb]:
                b.release(st["t"])
            return gb

        def logsig(z, n, ztok, tmp):
            t = ve.stt(tmp, z, -1.0, z, ALU.mult, ALU.max, ztok)
            t = sc.act(tmp, tmp, ACT.Exp, t, scale=-1.0)
            t = sc.act(tmp, tmp, ACT.Ln, t, bias=1.0)
            return ve.stt(z, z, 0.0, tmp, ALU.min, ALU.subtract, t)

        def narrow(w, name):
            wb = mk_blk(1)
            src = wb.a[:, 0:P].rearrange("p (c n) -> p c n", n=16)
            tl = load(po, name, src, w.rearrange("(c p) n -> p c n", p=P), wb.w)
            t1 = sc.act(w16h[:, :, :], src, ACT.Copy, tl, w16_free)
            t2 = ve.tt(w16l[:, :, :], src, w16h[:, :, :].bitcast(F32), ALU.subtract, t1, w16_free)
            wb.release([t2])
            g = gbank()
            for t in range(2):
                for kc in range(8):
                    a = (HT.hi[:, kc, t * P:t * P + P], HT.lo[:, kc, t * P:t * P + P])
                    o = GB[g][:, t * 16:t * 16 + 16]
                    pe.wait(t1, t2, HT.tok[kc], gfree[g])
                    pe.mm(o, a[0], w16h[:, kc, :], kc == 0, False, skip=True)
                    pe.mm(o, a[0], w16l[:, kc, :], False, False, skip=True)
                    tk = pe.mm(o, a[1], w16h[:, kc, :], False, kc == 7, skip=True, inc=(kc == 7))
            w16_free[:] = [tk]
            return g, tk

        w16_free = []

        def gla_layer(l):
            gb = bcast(l * 48 + 16, mod, mod_tok[l])
            modulated(l, 0)
            g, tk = narrow(I["gla_w_in_2"][0][:, 3072:3088], "w16a")
            ab_ = mk_blk(1)
            tc = ve.copy(ab_.a[:, 0:32], GB[g][:, 0:32], tk, ab_.w)
            gfree[g] = [tc]
            g = gbank()
            for t in range(2):
                tk = pe.tr(GB[g][0:16, t * P:t * P + P], ab_.a[:, t * 16:t * 16 + 16], ident[:, :], tc, gfree[g],
                           inc=(t == 1))
            aT = mk_blk(1)
            ta = ve.copy(aT.a[0:16, :], GB[g][0:16, 0:256], tk, aT.w)
            gfree[g] = [ta]
            ab_.release([tk])
            wg, bgt = mk_blk(2), mk_blk(2)
            tw = load(po, "wgu", wg.a[0:16, :], I["gla_w_gate_up_2"][0], wg.w)
            tb = load(po, "bgt", bgt.a, I["gla_b_gate_2"].to_broadcast([P, 512]), bgt.w)
            la = mk_blk(4)
            tl = []
            tmp = mk_blk(2)
            for t in range(2):
                g = gbank()
                tk = pe.mm(GB[g][:, :], aT.a[0:16, t * P:t * P + P], wg.a[0:16, :], True, True, ta, tw, gfree[g],
                           inc=True)
                z = la.a[:, t * 512:t * 512 + 512]
                t1 = ve.tt(z, GB[g][:, :], bgt.a, ALU.add, tk, tb, la.w, tmp.w)
                gfree[g] = [t1]
                tl.append(logsig(z, 512, t1, tmp.a))
                tmp.w = [tl[-1]]
            for b in (aT, wg, bgt, tmp):
                b.release([tl[-1], tk])
            la.tok = tl
            drain(lambda: not busy())
            dec, mk = mk_blk(5), mk_blk(4)
            td = load(po, "gd", dec.a[:, 0:1152], C["gladec"], dec.w)
            tmk = load(po, "gm", mk.a, C["glamask"], mk.w)
            qT, kT = mk_blk(4), mk_blk(4)
            gemm(HT, 0, ("gla", l, 0), D, "FF", ev_copy(qT, lambda g: quad(qT, g)))
            gemm(HT, 0, ("gla", l, 1), D, "FF", ev_copy(kT, lambda g: quad(kT, g)))
            st = {"n": 0, "t": []}
            V, R = [mk_blk(4), mk_blk(4)], [mk_blk(4), mk_blk(4)]

            def head(h):
                def task(sl):
                    q = qT.a[:, h * 256:h * 256 + 256]
                    k = kT.a[:, h * 256:h * 256 + 256]
                    psf = sl.ps[:, :, :].rearrange("p a b -> p (a b)")
                    ps8 = psf.rearrange("p (n c) -> p n c", n=8)
                    S8 = sl.S[:, 0:1024].rearrange("p (n c) -> p n c", n=8)
                    E = sl.S[:, 0:1024]
                    W = sl.W
                    kc0 = W[:, 1280:1536]
                    for t in range(2):
                        yield
                        for hf in range(2):
                            if hf == 0:
                                tk = pe.mm(sl.ps[:, 0, :], la.a[:, t * 512 + h * P:t * 512 + h * P + P],
                                           dec.a[:, 0:512], True, True, la.tok, td, sl.ps_free)
                            else:
                                pe.mm(sl.ps[:, 1, 0:384], la.a[:, t * 512 + h * P:t * 512 + h * P + P],
                                      dec.a[:, 512:896], True, True)
                                tk = pe.mm(sl.ps[:, 1, 384:512], la.a[:, t * 512 + h * P:t * 512 + h * P + P],
                                           dec.a[:, 896 + 128 * t:1024 + 128 * t], True, True, inc=True)
                        yield
                        te = sc.act(E, psf, ACT.Exp, tk, sl.S_free)
                        yield
                        qt = q[:, t * P:t * P + P]
                        kt = k[:, t * P:t * P + P]
                        KE = W[:, 0:1024].rearrange("p (n c) -> p n c", n=8)
                        t1 = po.tt(KE, S8, kt.unsqueeze(1).to_broadcast([P, 8, P]), ALU.mult, te, kT.tok, sl.W_free)
                        if t == 0:
                            t3 = po.copy(kc0[:, 0:P], KE[:, 7, :], t1)
                        t2 = ve.tt(S8, S8, qt.unsqueeze(1).to_broadcast([P, 8, P]), ALU.mult, te, t1, qT.tok)
                        yield
                        if t == 1:
                            tx_ = pe.mm(psf[:, 0:P], kc0[:, 0:P], S8[:, 7, :], True, True, t2, t3, inc=True)
                            tw01 = sc.act(kc0[:, P:2 * P], psf[:, 0:P], ACT.Copy, tx_, scale=128 ** -0.5)
                        for n in range(8):
                            lh, rh = (KE[:, n, :], S8[:, n, :]) if n < 7 else (kt, qt)
                            tk = pe.mm(ps8[:, n, :], lh, rh, True, True, t1, t2, tw01 if t == 1 else None,
                                       inc=(n == 7))
                        yield
                        tm = ve.tt(E, psf, mk.a, ALU.mult, tk, tmk)
                        tr_ = ve.red(W[:, 1024 + t * P:1024 + t * P + P], S8.rearrange("p n c -> p c n"), ALU.add, tm,
                                     sl.W_free)
                        sl.ps_free = [tm]
                        sl.S_free = [tr_]
                        sl.W_free = [tk, t3]
                    wt = [t1, tr_, tw01]
                    yield
                    vb = V[h // 2]

                    def v(t):
                        return vb.a[:, t * 512 + (h % 2) * 256:t * 512 + (h % 2) * 256 + 256]
                    drainable = R[h // 2]
                    pe.mm(psf[:, 0:256], W[:, 1024:1152], v(0), True, True, wt, vb.tok, sl.ps_free)
                    pe.mm(psf[:, 256:512], kc0[:, P:2 * P], v(0), True, False)
                    tk = pe.mm(psf[:, 256:512], W[:, 1152:1280], v(1), False, True, inc=True)
                    yield
                    ss = smc(2)
                    for t in range(2):
                        t1 = sc.act(E[:, t * 256:t * 256 + 256], psf[:, t * 256:t * 256 + 256], ACT.Square, tk, sl.S_free,
                                    accum=ss[:, t:t + 1])
                    rs, tr_ = rstd_of(ss, 2, 1.0 / 256, t1)
                    rs2 = smc(2)
                    t3 = ve.ts(rs2, rs, 0.5, None, ALU.mult, None, tr_)
                    yield
                    rb = R[h // 2]
                    for t in range(2):
                        ra = rb.a[:, t * 512 + (h % 2) * 256:t * 512 + (h % 2) * 256 + 256]
                        t4 = ve.stt(ra, psf[:, t * 256:t * 256 + 256], rs2[:, t:t + 1], ra, ALU.mult, ALU.mult,
                                    t3, t1, rb.tok)
                    sl.ps_free = [t4]
                    sl.W_free = [tk]
                    sl.S_free = [t1]
                    st["n"] += 1
                    st["t"].append(t4)
                return task

            for h in range(2):
                pend.append(head(h))
            gemm(HT, 0, ("gla", l, 2), D, "TT", ev_copy(V[0], lambda g: quad(V[0], g)))
            gemm(HT, 0, ("gla", l, 3), D, "TT", ev_copy(V[1], lambda g: quad(V[1], g)))
            gemm(HT, 0, ("gla", l, 4), D, "TT", lambda g, ps, t: silu2(quad(R[0], g), ps[:, :], t, R[0]))
            gemm(HT, 0, ("gla", l, 5), D, "TT", lambda g, ps, t: silu2(quad(R[1], g), ps[:, :], t, R[1]))
            for h in range(2, 4):
                pend.append(head(h))
            drain(lambda: not busy())
            for b in V + [qT, kT, la, dec, mk]:
                b.release(st["t"])
            hn = cols[:, COL["head"]:COL["head"] + 2]
            for i in range(2):
                rel = to_T(R[i].a.rearrange("p (t e) -> p t e", t=2), st["t"], Sub(OT, 4 * i), scol=hn, ctok=tcols,
                           nk=4, hn=True)
                R[i].release(rel)
            return gb

        def fox_layer(l):
            gb = bcast(l * 48 + 16, mod, mod_tok[l])
            modulated(l, 0)
            g, tk = narrow(I["fox_w_in_2"][0][:, 3072:3088], "w16b")
            fb = mk_blk(1)
            z, bf, tp = fb.a[:, 0:32], fb.a[:, 32:64], fb.a[:, 64:96]
            cb = mk_blk(3)
            cum, msk = cb.a[:, 0:512], cb.a[:, 512:768]
            tcm = load(po, "cum", cum, C["cum"], cb.w)
            tmk = load(po, "fm", msk, C["foxmask"], cb.w)
            tbf = load(po, "bf", bf[:, 0:16], I["fox_b_f_2"].to_broadcast([P, 16]), fb.w)
            for t in range(2):
                t1 = ve.tt(z[:, t * 16:t * 16 + 16], GB[g][:, t * 16:t * 16 + 16], bf[:, 0:16], ALU.add, tk, tbf, fb.w)
            gfree[g] = [t1]
            tz = logsig(z, 32, t1, tp)
            lq = fb.a[:, 96:128]
            g = gbank()
            for t in range(2):
                for jj in range(t + 1):
                    tk = pe.mm(GB[g][:, t * 16:t * 16 + 16], cum[:, jj * 256 + t * P:jj * 256 + t * P + P],
                               z[:, jj * 16:jj * 16 + 16], jj == 0, jj == t, tz, tcm, gfree[g],
                               inc=(t == 1 and jj == t))
            tlq = ve.copy(lq, GB[g][:, 0:32], tk)
            gfree[g] = [tlq]
            z8 = fb.a[:, 128:160]
            tz8 = ve.ts(z8, z, -8.0, None, ALU.mult, None, tz)
            st = {"n": 0, "t": []}
            rel_list = []
            for b in range(8):
                OT.tok[b] = []

            def head4(h0, t, qb, kb, vb):
                def task(sl):
                    K = (t + 1) * P
                    yield
                    for n in range(4):
                        h = h0 + ORD[n]
                        p0, bl = 64 * (h % 2), (h // 2) % 4
                        o = sl.ps[:, n // 2, (n % 2) * 256:(n % 2) * 256 + K]
                        pe.mm(o, qb.a[p0:p0 + 64, bl * 256 + t * P:bl * 256 + t * P + P],
                              kb.a[p0:p0 + 64, bl * 256:bl * 256 + K], True, False, qb.tok, kb.tok, tz8, tcm,
                              sl.ps_free, skip=True)
                        for jj in range(t + 1):
                            tk = pe.mm(o, z8[:, jj * 16 + h:jj * 16 + h + 1].to_broadcast([P, P]),
                                       cum[:, jj * 256:jj * 256 + K], False, jj == t, inc=(n == 3 and jj == t),
                                       skip=True)
                    yield
                    S3 = sl.S[:, 0:4 * 257].rearrange("p (n k) -> p n k", n=4)
                    p4 = sl.ps[:, :, :].rearrange("p a (b k) -> p (a b) k", b=2)
                    for n in range(4):
                        h = h0 + ORD[n]
                        t1 = ve.ts(S3[:, n, 0:K], p4[:, n, 0:K], 0.125, lq[:, t * 16 + h:t * 16 + h + 1], ALU.mult,
                                   ALU.add, tk, tlq, sl.S_free)
                    t2 = ve.tt(S3[:, :, 0:K], S3[:, :, 0:K], msk[:, 256 - K:256].unsqueeze(1).to_broadcast([P, 4, K]),
                               ALU.add, t1, tmk)
                    nm = smc(4)
                    tn = ve.red(nm, S3[:, :, 0:K], ALU.max, t2, negate=True)

                    def v_of(kc, hp, n=None):
                        return None
                    yield from fox_pv(sl, t, S3, K, t2, tn, nm, vb, h0)
                    st["n"] += 1
                    st["t"] += [sl.ps_free[0]]
                return task

            def fox_pv(sl, t, S3, K, tv, tn, nm, vb, h0):
                nk = t + 1
                su = smc(4)
                te = exps(None, [S3[:, n, 0:K] for n in range(4)], nm, su, tn, tv)
                yield
                rc = smc(4)
                t1 = ve.recip(rc, su, te)
                for n in range(4):
                    t2 = ve.ts(S3[:, n, 0:K], S3[:, n, 0:K], rc[:, n:n + 1], None, ALU.mult, None, t1, te)
                yield
                psf = sl.ps[:, :, :].rearrange("p a b -> p (a b)")
                for kc in range(nk):
                    for n in range(4):
                        tk = pe.tr(psf[:, (kc * 4 + n) * P:(kc * 4 + n) * P + P], S3[:, n, kc * P:kc * P + P],
                                   ident[:, :], t2, inc=(kc == nk - 1 and n == 3))
                sl.S_free = [tk]
                yield
                tw = [sc.act(sl.W[:, 0:512], sl.ps[:, 0, :], ACT.Copy, tk, sl.W_free)]
                if nk == 2:
                    tw.append(ve.copy(sl.W[:, 512:1024], sl.ps[:, 1, :], tk, sl.W_free))
                yield
                W = sl.W[:, 0:1024].rearrange("p (k n q) -> p k n q", k=2, n=4)
                for n in range(4):
                    h = (h0 + ORD[n]) % 8
                    for kc in range(nk):
                        o = sl.ps[64 * (n // 2):64 * (n // 2) + 64, 0, (n % 2) * P:(n % 2) * P + P]
                        tk = pe.mm(o, vb.a[:, kc * 512 + h * 64:kc * 512 + h * 64 + 64], W[:, kc, n, :], kc == 0,
                                   kc == nk - 1, tw, vb.tok, inc=(n == 3 and kc == nk - 1), skip=True)
                sl.W_free = [tk]
                yield
                ob = h0 // 2
                o = sl.ps[:, 0, 0:256].rearrange("p (n q) -> p n q", n=2)
                tt_ = split_ps(OT.hi[:, ob:ob + 2, t * P:t * P + P], OT.lo[:, ob:ob + 2, t * P:t * P + P], o,
                               OT.waits(ob, 2), tk)
                for b in (ob, ob + 1):
                    OT.tok[b] = OT.tok[b] + tt_
                sl.ps_free = [tt_[-1]]

            for u in range(2):
                qb, kb, vb = mk_blk(4), mk_blk(4), mk_blk(4)
                gemm(HT, 0, ("fox", l, u), D, "FF", ev_copy(qb, lambda g: quad(qb, g)))
                gemm(HT, 0, ("fox", l, 2 + u), D, "FF", ev_copy(kb, lambda g: quad(kb, g)))
                gemm(HT, 0, ("fox", l, 4 + u), D, "TT", ev_copy(vb, lambda g: quad(vb, g)))
                rel_list += [qb, kb, vb]
                for h0 in (8 * u, 8 * u + 4):
                    for t in range(2):
                        pend.append(head4(h0, t, qb, kb, vb))
            drain(lambda: not busy())
            for b in rel_list + [fb, cb]:
                b.release(st["t"])
            return gb

        def ffn(l):
            gb = bcast(l * 48 + 40, mod, mod_tok[l])
            modulated(l, 1)
            dacc_wait = [slots[0].ps_free + slots[1].ps_free]

            def down(v):
                b0 = 2 * (v % 4)
                for kc in range(2):
                    s, wt = take(("dn", l, v))
                    pe.wait(wt, OT.tok[b0 + kc])
                    if v == 0 and kc == 0:
                        pe.wait(dacc_wait[0])
                    for t in range(2):
                        a = (OT.hi[:, b0 + kc, t * P:t * P + P], OT.lo[:, b0 + kc, t * P:t * P + P])
                        for n in range(2):
                            o = AB[t][:, n, :]
                            pe.mm(o, a[0], whi[:, s, n, :], v == 0 and kc == 0, False, skip=True)
                            pe.mm(o, a[0], wlo[:, s, n, :], False, False, skip=True)
                            tk = pe.mm(o, a[1], whi[:, s, n, :], False, v == 10 and kc == 1, skip=True,
                                       inc=(t == 1 and n == 1))
                    spl_free[s] = [tk]
                    OT.free[b0 + kc] = [tk]
                return tk

            for v in range(12):
                if v < 11:
                    b0 = 2 * (v % 4)
                    tmp = mk_blk(4)
                    t1_, t2_ = tmp.a[:, 0:512], tmp.a[:, 512:1024]
                    keep = {}

                    def ev(g, ps, t):
                        if g == 0:
                            ta = sc.act(t1_, ps[:, :], ACT.Tanh, t, tmp.w, scale=0.5)
                            keep["t"] = ve.stt(t1_, t1_, 1.0, ps[:, :], ALU.add, ALU.mult, ta)
                            return [keep["t"]]
                        tb = ve.stt(t2_, t1_, 0.5, ps[:, :], ALU.mult, ALU.mult, t, keep["t"], tmp.w)
                        hi = OT.hi[:, b0:b0 + 2, :].rearrange("p a c -> p (a c)")
                        lo = OT.lo[:, b0:b0 + 2, :].rearrange("p a c -> p (a c)")
                        th = sc.act(hi, t2_, ACT.Copy, tb, OT.waits(b0, 2))
                        tl = po.tt(lo, t2_, hi.bitcast(F32), ALU.subtract, tb, th, OT.waits(b0, 2))
                        OT.write(b0, 2, [th, tl])
                        keep["r"] = [th, tl]
                        return [tb]
                    gemm(HT, 0, ("gu", l, v), D, "FF", ev)
                    tmp.release(keep["r"])
                if v > 0:
                    tk = down(v - 1)
            nx, fr = [], [[], []]
            for t in range(2):
                for n in range(2):
                    fr[t] += residual(gb, n, nx)(t, AB[t][:, n, :], tk)
                slots[t].ps_free = fr[t]
            xtok[:] = nx
            gb.release(nx)

        for l in range(2):
            layer1(l)
        xtok[:] = final_norm(COL["g_final"], X)
        ada_sums()
        for l in range(4):
            gb = (swa_layer, gla_layer, fox_layer)[l % 3](l)
            nx = []
            for u in range(2):
                gemm(OT, 0, ("wo2", l, u), D, "TT", residual(gb, u, nx))
            gb.release(nx)
            xtok[:] = nx
            ffn(l)
        assert state["piece"] == len(stream) and not halves, (state, len(halves))
        tf = final_norm(COL["f_norm"], X)
        tout = load(sp, "out", out[0].rearrange("(t p) d -> p t d", p=P), X[:, :, :], tf)
        sp.wait(tout, tscr)

        block = ctx.enter_context(nc.Block())

        def run(q):
            def f(eng):
                own = sems.get(q.key)
                for op in q.ops:
                    if op[0] == "wait":
                        eng.wait_ge(sems[op[1]], op[2])
                    elif op[0] == "dma":
                        eng.dma_start(op[1], op[2]).then_inc(sems[op[3]], 16)
                    else:
                        ins = op[1](eng)
                        if op[2]:
                            ins.then_inc(own, 1)
            return f

        block.tensor(run(pe))
        block.scalar(run(sc))
        block.vector(run(ve))
        block.gpsimd(run(po))
        block.sync(run(sp))


_INS = ['x', 'mem', 'g_norm', 'w_in', 'diff_lambda', 'w_mem_kv', 'g_mem', 'w_br_diff', 'w_br_dil', 'w_br_mem',
        'w_out', 'rel_bias', 'g_final', 'c_2', 'ada_w_2', 'ada_b_2', 'norm_gain_2', 'ffn_w_gu_2', 'ffn_w_down_2',
        'swa_w_in_2', 'swa_sinks_2', 'swa_w_o_2', 'gla_w_in_2', 'gla_w_gate_up_2', 'gla_b_gate_2',
        'gla_head_norm_2', 'gla_w_o_2', 'fox_w_in_2', 'fox_b_f_2', 'fox_w_o_2', 'final_norm_2']


def kernel(**inputs):
    import numpy as _np
    import concourse.bacc as _bacc
    from concourse.bass_utils import run_bass_kernel_spmd as _run

    nc = _bacc.Bacc("TRN2", target_bir_lowering=False, num_devices=1)
    arrays, ins, cst = {}, {}, {}
    for name in _INS:
        a = _np.ascontiguousarray(inputs[name])
        arrays[f"in_{name}"] = a
        ins[name] = nc.dram_tensor(f"in_{name}", a.shape, F32, kind="ExternalInput").ap()
    for name, a in constants().items():
        arrays[f"c_{name}"] = a
        cst[name] = nc.dram_tensor(f"c_{name}", a.shape, F32, kind="ExternalInput").ap()
    out = nc.dram_tensor("out", (1, T, D), F32, kind="ExternalOutput").ap()
    program(nc, ins, cst, out)
    r = _run(nc, [arrays], core_ids=[0])
    return r.results[0]["out"]
```

```python
import math
from contextlib import ExitStack

import numpy as np
import concourse.bass as bass
from concourse import mybir

F32 = mybir.dt.float32
F32R = mybir.dt.float32r
ALU = mybir.AluOpType
ACT = mybir.ActivationFunctionType
AXX = mybir.AxisListType.X

P = 128
D = 1024
T = 256
N_IN = 13312
DFF = 2816
EPS = 1e-6
OFF = dict(dq=0, dk=1024, dv=2048, dg=3072, lq=4096, lk=5632, lv=7168, lg=8704, mq=9216, mg=9728,
           mgate=10240)
NEG = -1e30


def bucket(rel):
    half, max_exact = 16, 8
    ret = np.where(rel > 0, half, 0)
    n = np.abs(rel)
    nf = np.maximum(n, 1).astype(np.float32)
    large = max_exact + (np.log(nf / np.float32(max_exact)) / np.float32(math.log(1024 / max_exact))
                         * np.float32(half - max_exact)).astype(np.int32)
    return ret + np.where(n < max_exact, n, np.minimum(large, half - 1))


def constants():
    c = {}
    i = np.arange(P)
    c["ident"] = np.eye(P, dtype=np.float32)
    rel = np.arange(512) - 255
    oh = (bucket(rel)[None, :] == np.arange(32)[:, None]).astype(np.float32)
    c["onehot"] = oh
    dm = np.zeros((20, 512), np.float32)
    dm[8:12] = np.where(np.abs(rel) <= 64, 0, NEG)
    dm[12:16] = np.where(rel % 4 == 0, 0, NEG)
    dm[16:20] = np.where(rel % 16 == 0, 0, NEG)
    c["dilmask"] = dm
    inv = (1.0 / (np.float32(150000.0) ** (np.arange(0, 64, 2, dtype=np.float32) / np.float32(64)))
           ).astype(np.float32)
    ang = np.arange(T, dtype=np.float32)[:, None] * inv[None, :]
    cos, sin = np.cos(ang).astype(np.float32), np.sin(ang).astype(np.float32)
    cs = np.stack([np.concatenate([cos, cos], 1), np.concatenate([-sin, sin], 1)])
    c["rope"] = np.ascontiguousarray(cs.reshape(2, 2, P, 64).transpose(2, 0, 1, 3)).reshape(P, 256)
    tri = np.where(i[None, :] <= i[:, None], 0, NEG).astype(np.float32)
    prev = np.where(i[None, :] > i[:, None], 0, NEG).astype(np.float32)
    c["swamask"] = np.concatenate([prev, tri], 1)
    c["foxmask"] = np.concatenate([np.zeros((P, P), np.float32), tri], 1)
    dl = np.zeros((P, 9, P), np.float32)
    mk = np.zeros((P, 8, P), np.float32)
    for l in range(7):
        h = 64 >> l
        for t in range(P):
            mid = t // (2 * h) * 2 * h + h
            if t >= mid:
                dl[mid:t + 1, l, t] = 1
                mk[mid - h:mid, l, t] = 1
            else:
                dl[t + 1:mid, l, t] = 1
    dl[:, 7, :] = i[:, None] > i[None, :]
    dl[:, 8, :] = i[:, None] <= i[None, :]
    mk[:, 7, :] = np.eye(P)
    c["gladec"] = (dl / 16).reshape(P, 9 * P)
    c["glamask"] = (mk * np.float32(128 ** -0.5)).reshape(P, 8 * P)
    j = np.arange(T)
    up = (j[:, None] <= j[None, :]).astype(np.float32)
    c["cum"] = np.ascontiguousarray(up.reshape(2, P, T).transpose(1, 0, 2)).reshape(P, 512)
    return {k: np.ascontiguousarray(v, dtype=np.float32) for k, v in c.items()}


class Q:

    def __init__(self, key):
        self.key, self.n, self.ops, self.seen = key, 0, [], {}

    def wait(self, *toks):
        for t in toks:
            if t is None:
                continue
            if isinstance(t, list):
                self.wait(*t)
                continue
            k, v = t
            if self.seen.get(k, 0) < v:
                self.seen[k] = v
                self.ops.append(("wait", k, v))

    def do(self, fn, *waits, inc=True):
        self.wait(*waits)
        self.ops.append(("do", fn, inc))
        if inc:
            self.n += 1
            return (self.key, self.n)
        return None

    def dma(self, out, in_, key, count, *waits):
        self.wait(*waits)
        self.ops.append(("dma", out, in_, key))
        return (key, count)

    def mm(self, out, lhsT, rhs, start, stop, *waits, inc=False, skip=False):
        return self.do(lambda e: e.matmul(out, lhsT, rhs, start=start, stop=stop, skip_group_check=skip),
                       *waits, inc=inc)

    def tr(self, out, in_, ident, *waits, inc=False):
        return self.do(lambda e: e.transpose(out, in_, ident), *waits, inc=inc)

    def act(self, out, in_, func, *waits, bias=0.0, scale=1.0, accum=None):
        return self.do(lambda e: e.activation(out, in_, func, bias=bias, scale=scale, accum_out=accum), *waits)

    def copy(self, out, in_, *waits):
        return self.do(lambda e: e.tensor_copy(out, in_), *waits)

    def tt(self, out, a, b, op, *waits):
        return self.do(lambda e: e.tensor_tensor(out, a, b, op), *waits)

    def ts(self, out, a, s1, s2, op0, op1, *waits):
        if s2 is None:
            return self.do(lambda e: e.tensor_scalar(out, a, s1, None, op0), *waits)
        return self.do(lambda e: e.tensor_scalar(out, a, s1, s2, op0, op1), *waits)

    def stt(self, out, a, s, b, op0, op1, *waits):
        return self.do(lambda e: e.scalar_tensor_tensor(out=out, in0=a, scalar=s, in1=b, op0=op0, op1=op1), *waits)

    def red(self, out, in_, op, *waits, negate=False):
        return self.do(lambda e: e.tensor_reduce(out, in_, AXX, op, negate=negate), *waits)

    def recip(self, out, in_, *waits):
        return self.do(lambda e: e.reciprocal(out, in_), *waits)

    def memset(self, ap, v, *waits):
        return self.do(lambda e: e.memset(ap, v), *waits)


NRAW = 6
NSPL = 5
LOOK = 3


def program(nc, I, C, out):
    pe, sc, ve, po, sp = Q("pe"), Q("sc"), Q("ve"), Q("po"), Q("sp")
    with ExitStack() as ctx:
        def sb(name, shape, dt=F32):
            return ctx.enter_context(nc.sbuf_tensor(name, shape, dt))

        sems = {k: ctx.enter_context(nc.semaphore("s_" + k)) for k in ("pe", "sc", "ve", "po")}

        def sem(name):
            sems[name] = ctx.enter_context(nc.semaphore("s_" + name))
            return name

        raw = sb("raw", [P, NRAW, 4, 512])
        whi = sb("whi", [P, NSPL, 2, 512], F32R)
        wlo = sb("wlo", [P, NSPL, 2, 512], F32R)
        X = sb("X", [P, 2, D])

        class TA:

            def __init__(self, n):
                self.hi = sb(n + "h", [P, 8, T], F32R)
                self.lo = sb(n + "l", [P, 8, T], F32R)
                self.tok = [[] for _ in range(8)]
                self.free = [[] for _ in range(8)]

            def write(self, b0, nb, toks):
                for b in range(b0, b0 + nb):
                    self.tok[b] = toks

            def waits(self, b0, nb):
                return [t for b in range(b0, b0 + nb) for t in self.free[b]]

        HT, OT = TA("HT"), TA("OT")
        NB = 45
        pool = sb("pool", [P, NB, 256])
        bias_t = sb("bias_t", [P, 6, 384])
        ident = sb("ident_t", [P, P])
        cols = sb("cols", [P, P])
        adb = sb("adb", [P, 192])
        mod = sb("mod", [P, 192])
        SM = 320
        sm = sb("sm", [P, SM])
        c8 = sb("c8", [P, 8])
        ones = sb("ones", [P, 1])
        mhalf = sb("mhalf", [P, 16])
        nlam = sb("nlam", [P, 2])
        w16h = sb("w16h", [P, 8, 16], F32R)
        w16l = sb("w16l", [P, 8, 16], F32R)
        scratch = nc.dram_tensor("bias_scratch", (20, P, 512), F32, kind="Internal").ap()

        GB = [ctx.enter_context(nc.psum_tensor(f"G{i}", [P, 512], F32)) for i in range(4)]
        AB = [ctx.enter_context(nc.psum_tensor(f"A{i}", [P, 2, 512], F32)) for i in range(2)]

        class Slot:
            def __init__(self, j):
                self.j, self.ps, self.ps_free = j, AB[j], []
                self.S, self.S_free = sb(f"S{j}", [P, 1040]), []
                self.W, self.W_free = sb(f"W{j}", [P, 1536]), []

        slots = [Slot(0), Slot(1)]

        class Half:

            def __init__(self, s, k):
                self.j = 2 * s.j + k
                self.ps, self.S, self.W = s.ps[:, k, :], s.S[:, 520 * k:520 * k + 514], s.W[:, 768 * k:768 * k + 512]
                self.ps_free, self.S_free, self.W_free = s.ps_free, s.S_free, s.W_free

        class Extra:

            def __init__(self, j):
                self.j, self.g, self.b = j, gbank(), [Blk(3), Blk(2)]
                self.ps, self.S, self.W = GB[self.g], self.b[0].a[:, 0:514], self.b[1].a
                self.ps_free, self.S_free, self.W_free = gfree[self.g], self.b[0].w, self.b[1].w

            def close(self):
                gfree[self.g] = self.ps_free
                self.b[0].release(self.S_free)
                self.b[1].release(self.W_free)

        gfree = [[] for _ in range(4)]
        gnext = [0]

        def gbank():
            g = gnext[0] % 4
            gnext[0] += 1
            return g

        pfree = [[] for _ in range(NB)]
        pbusy = [False] * NB

        class Blk:

            def __init__(self, n):
                fit = [k for k in range(NB - n + 1) if not any(pbusy[k:k + n])]
                for k in fit[::-1] if n < 4 else fit:
                    break
                else:
                    raise MemoryError(f"pool: {n} wanted, busy {sum(pbusy)}")
                self.k, self.n = k, n
                self.w = [t for j in range(k, k + n) for t in pfree[j]]
                pbusy[k:k + n] = [True] * n
                self.a = pool[:, k:k + n, :].rearrange("p n c -> p (n c)")
                self.tok = []

            def release(self, toks):
                for j in range(self.k, self.k + self.n):
                    pbusy[j] = False
                    pfree[j] = list(toks)

        smn = [0]

        def smc(n):
            if smn[0] % SM + n > SM:
                smn[0] += SM - smn[0] % SM
            a = smn[0] % SM
            smn[0] += n
            return sm[:, a:a + n]

        pend, live, place = [], [None] * 2, list(slots)

        def halve():
            assert not busy()
            place[:] = [Half(s, k) for s in slots for k in range(2)]
            live[:] = [None] * 4

        def widen(n):
            place.extend(Extra(len(place) + i) for i in range(n))
            live.extend([None] * n)

        def whole():
            assert not busy()
            for h in place[4:]:
                h.close()
            del place[4:]
            for s in slots:
                hs = [h for h in place if h.j // 2 == s.j]
                s.ps_free, s.S_free, s.W_free = ([t for h in hs for t in free_of(h)[i]] for i in range(3))
            place[:] = slots
            live[:] = [None] * 2

        def free_of(h):
            return h.ps_free, h.S_free, h.W_free

        age = [0]

        def step():
            started = 0
            for j in range(len(place)):
                if live[j] is None and pend:
                    age[0] += 1
                    live[j] = (age[0], pend.pop(0)(place[j]))
                    started += 1
                    if started * 2 >= len(place):
                        break
            for a, j in sorted(((live[j][0], j) for j in range(len(place)) if live[j]), reverse=True):
                try:
                    next(live[j][1])
                except StopIteration:
                    live[j] = None

        def busy():
            return bool(pend) or any(x is not None for x in live)

        def mk_blk(n):
            while True:
                fits = any(not any(pbusy[k:k + n]) for k in range(NB - n + 1))
                if fits and (pbusy.count(False) >= n + 2 or not busy()):
                    return Blk(n)
                if not busy():
                    raise MemoryError(f"{n} of " + "".join("#" if b else "." for b in pbusy))
                step()

        def drain(cond):
            while not cond():
                if not busy():
                    raise MemoryError("".join("#" if b else "." for b in pbusy))
                step()

        def cseg(w, r0, nk, segs):
            res, at = [], 0
            for c0, n in segs:
                res.append((at, n, w[r0:r0 + nk * P, c0:c0 + n].rearrange("(c p) n -> p c n", p=P)))
                at += n
            return res

        def unit(key, w, K, segs):
            return [("w", key, cseg(w, k * 512, 4, segs)) for k in range(K // 512)]

        def mkv(l):
            for u in range(2):
                yield from unit(("mkv", l, u), I["w_mem_kv"][l], D, [(u * 512, 512)])

        def plan():
            for l in range(2):
                wi = I["w_in"][l]
                if l == 0:
                    yield from mkv(0)
                yield from unit(("mq", l), wi, D, [(OFF["mq"], 512)])
                yield from unit(("mg", l), wi, D, [(OFF["mg"], 512)])
                for pr in range(2):
                    def g(o, gi):
                        return (OFF[o] + gi * 512 + pr * 256, 256)
                    yield from unit(("dil", l, pr, 0), wi, D, [g("lq", 0), g("lq", 1)])
                    yield from unit(("dil", l, pr, 1), wi, D, [g("lq", 2), g("lk", 2)])
                    yield from unit(("dil", l, pr, 2), wi, D, [g("lk", 0), g("lk", 1)])
                    yield from unit(("dil", l, pr, 3), wi, D, [g("lv", 0), g("lv", 1)])
                    yield from unit(("dil", l, pr, 4), wi, D, [g("lv", 2), (OFF["lg"] + pr * 256, 256)])
                for u in range(2):
                    yield from unit(("gate", l, 2, u), wi, D, [(OFF["mgate"] + 2048 + u * 512, 512)])
                    yield from unit(("ym", l, u), I["w_br_mem"][l], 512, [(u * 512, 512)])
                for hf in range(2):
                    yield from unit(("diff", l, hf, 0), wi, D, [(hf * 256, 256), (512 + hf * 256, 256)])
                    yield from unit(("diff", l, hf, 1), wi, D,
                                    [(1024 + hf * 256, 256), (1536 + hf * 256, 256)])
                    yield from unit(("diff", l, hf, 2), wi, D, [(2048 + hf * 512, 512)])
                    yield from unit(("diff", l, hf, 3), wi, D, [(3072 + hf * 512, 512)])
                for u in range(2):
                    yield from unit(("gate", l, 1, u), wi, D, [(OFF["mgate"] + 1024 + u * 512, 512)])
                    yield from unit(("yb", l, u), I["w_br_dil"][l], 512, [(u * 512, 512)])
                if l == 0:
                    yield from mkv(1)
                for u in range(2):
                    yield from unit(("gate", l, 0, u), wi, D, [(OFF["mgate"] + u * 512, 512)])
                for u in range(2):
                    yield from unit(("ya", l, u), I["w_br_diff"][l], D, [(u * 512, 512)])
                for u in range(2):
                    yield from unit(("wo", l, u), I["w_out"][l], D, [(u * 512, 512)])
            for l in range(4):
                kind, j = l % 3, l // 3
                if kind == 0:
                    for u in (2, 0, 1):
                        yield from unit(("swa", l, u), I["swa_w_in_2"][j], D, [(u * 512, 512)])
                    wo = I["swa_w_o_2"][j]
                elif kind == 1:
                    for u in range(6):
                        yield from unit(("gla", l, u), I["gla_w_in_2"][j], D, [(u * 512, 512)])
                    wo = I["gla_w_o_2"][j]
                else:
                    for u in (0, 2, 4, 1, 3, 5):
                        yield from unit(("fox", l, u), I["fox_w_in_2"][j], D, [(u * 512, 512)])
                    wo = I["fox_w_o_2"][j]
                for u in range(2):
                    yield from unit(("wo2", l, u), wo, D, [(u * 512, 512)])
                for u in range(12):
                    if u < 11:
                        yield from unit(("gu", l, u), I["ffn_w_gu_2"][l], D, [(u * 256, 256), (DFF + u * 256, 256)])
                    if u > 0:
                        v = u - 1
                        wd = I["ffn_w_down_2"][l][v * 256:v * 256 + 256, :]
                        yield ("w", ("dn", l, v), [("dn", 0, wd.rearrange("(c p) n -> p c n", p=P))])

        def full_plan():
            def ada(*ls):
                return [("ada", (l, u, k), cseg(I["ada_w_2"][l], k * 512, 4, [(u * 512, 512)]))
                        for l in ls for u in range(12) for k in range(2)]

            def spread(main, extra, skip, end):
                gave = 0
                for i, m in enumerate(main):
                    yield m
                    want = min(len(extra), max(0, i - skip + 1) * len(extra) // (len(main) - skip - end))
                    while gave < want:
                        yield extra[gave]
                        gave += 1

            main = list(plan())
            one = [m for m in main if m[1][0] in FIRST]
            yield from spread(one, ada(0, 1), 6, 12)
            for l in range(4):
                extra = (ada(2) + ada(3)[:8], ada(3)[8:], [], [])[l]
                yield from spread([m for m in main if m[1][0] not in FIRST and m[1][1] == l], extra,
                                  (2, 17, 0, 0)[l], 3)

        FIRST = {"mkv", "mq", "mg", "dil", "gate", "ym", "diff", "yb", "ya", "wo"}
        stream = list(full_plan())
        for i in range(NRAW):
            sem(f"raw{i}")
        raw_free = [[] for _ in range(NRAW)]
        raw_cnt = [0] * NRAW
        spl_free = [[] for _ in range(NSPL)]
        state = {"piece": 0, "half": 0}
        halves = []
        adaq = []

        acc_blk = {}

        def fetch():
            i = state["piece"]
            state["piece"] += 1
            kind, key, segs = stream[i]
            r = i % NRAW
            rw = raw[:, r, :, :]
            for at, n, src in segs:
                if at == "dn":
                    dst = rw.rearrange("p (c a) n -> p c (a n)", a=2)
                else:
                    dst = rw[:, :, at:at + n]
                raw_cnt[r] += 16
                ld = sp.dma(dst, src, f"raw{r}", raw_cnt[r], raw_free[r])
            if kind == "w":
                toks = []
                for h in range(2):
                    s = state["half"] % NSPL
                    state["half"] += 1
                    src = rw[:, 2 * h:2 * h + 2, :]
                    th = sc.act(whi[:, s], src, ACT.Copy, ld, spl_free[s])
                    tl = ve.tt(wlo[:, s], src, whi[:, s].bitcast(F32), ALU.subtract, ld, th, spl_free[s])
                    toks.append(tl)
                    halves.append((key, s, [th, tl]))
                raw_free[r] = [toks[-1]]
            else:
                l, u, k = key
                if k == 0:
                    acc_blk[0] = mk_blk(2)
                b = acc_blk[0]
                t = None
                for c in range(4):
                    cc = c8[:, 4 * k + c:4 * k + c + 1]
                    if k == 0 and c == 0:
                        t = ve.ts(b.a, rw[:, c, :], cc, None, ALU.mult, None, ld, tc8, b.w)
                    else:
                        t = ve.stt(b.a, rw[:, c, :], cc, b.a, ALU.mult, ALU.add, ld, t or b.tok)
                    b.tok = [t]
                raw_free[r] = [t]
                if k == 1:
                    adaq.append((l, u, b))

        def ada_sums():
            while adaq:
                l, u, b = adaq.pop(0)
                g = gbank()
                for n in range(4):
                    t = pe.mm(GB[g][:, n:n + 1], b.a[:, n * P:n * P + P], ones[:, :], True, True,
                              gfree[g], b.tok, tconst, inc=(n == 3))
                b.release([t])
                m = l * 48 + u * 4
                tv = ve.tt(mod[:, m:m + 4], GB[g][:, 0:4], adb[:, m:m + 4], ALU.add, t, tadb)
                gfree[g] = [tv]
                mod_tok[l] = tv

        mod_tok = {}
        deferred = []

        def take(key, ahead=True):
            while ahead and len(halves) < LOOK + 1 and state["piece"] < len(stream):
                fetch()
            k, s, t = halves.pop(0)
            assert k == key, (k, key)
            return s, t

        def gemm(A, b0, key, K, modes, evac, last=False):
            gs = [gbank(), gbank()]
            nk = K // P
            for kk in range(0, nk, 2):
                s, wt = take(key, ahead=not (last and kk == nk - 2))
                pe.wait(wt, [t for b in range(b0 + kk, b0 + kk + 2) for t in A.tok[b]])
                if kk == 0:
                    pe.wait(gfree[gs[0]])
                    if modes != "TT":
                        pe.wait(gfree[gs[1]])
                todo = []
                for i in range(2):
                    kc, kb = kk + i, b0 + kk + i
                    fst, lst = kc == 0, kc == nk - 1
                    if modes == "TT":
                        for t in range(2):
                            o = GB[gs[t]][:, :]
                            a = (A.hi[:, kb, t * P:t * P + P], A.lo[:, kb, t * P:t * P + P])
                            w = (whi[:, s, i, :], wlo[:, s, i, :])
                            todo += [(t, o, a[0], w[0], fst, False), (t, o, a[0], w[1], False, False),
                                     (t, o, a[1], w[0], False, lst)]
                    else:
                        for hf in range(2):
                            for q in range(2):
                                o = GB[gs[hf]][:, q * 256:q * 256 + 256]
                                if modes[hf] == "F":
                                    c = hf * 256 + q * P
                                    a = (whi[:, s, i, c:c + P], wlo[:, s, i, c:c + P])
                                    w = (A.hi[:, kb, :], A.lo[:, kb, :])
                                else:
                                    a = (A.hi[:, kb, q * P:q * P + P], A.lo[:, kb, q * P:q * P + P])
                                    w = (whi[:, s, i, hf * 256:hf * 256 + 256],
                                         wlo[:, s, i, hf * 256:hf * 256 + 256])
                                f = fst and q == 0
                                todo += [(hf, o, a[0], w[0], f, False), (hf, o, a[0], w[1], False, False),
                                         (hf, o, a[1], w[0], False, lst)]
                if modes == "TT":
                    todo.sort(key=lambda z: z[0])
                second = False
                for n, (bk, o, a, w, f, e) in enumerate(todo):
                    if bk == 1 and not second and kk == 0:
                        pe.wait(gfree[gs[1]])
                        second = True
                    end0 = modes == "TT" and kk == nk - 2 and n == len(todo) // 2 - 1
                    t = pe.mm(o, a, w, f, e, inc=(n == len(todo) - 1 or end0), skip=True)
                    if end0:
                        gfree[gs[0]] = evac(0, GB[gs[0]], t)
                spl_free[s] = [t]
                if kk == 2 and deferred:
                    deferred.pop()()
                if kk % 4 == 2:
                    if kk == nk - 2:
                        for b in range(b0, b0 + nk):
                            A.free[b] = [t]
                        for g in range(modes == "TT", 2):
                            gfree[gs[g]] = evac(g, GB[gs[g]], t)
                    ada_sums()
                step()
            return t

        def load(eng, name, dst, src, *waits):
            sem(name)
            return eng.dma(dst, src, name, 16, *waits)

        memb = mk_blk(8)
        tmem = load(sp, "mem0", memb.a.rearrange("p (t d) -> p t d", t=2),
                    I["mem"][0].rearrange("(t p) d -> p t d", p=P), memb.w)
        vrows = mk_blk(1)
        vr = vrows.a[:, 0:P]
        tid = load(sp, "id", ident[:, :], C["ident"])
        sem("vr")
        tv0 = ve.memset(vr, 0.0)
        nv = 0

        def vload(dst, src, *w):
            vr_cnt[0] += 16
            return sp.dma(dst, src, "vr", vr_cnt[0], *w)

        vr_cnt = [0]
        vload(vr[0:16, :], I["g_norm"].rearrange("l (a p) -> (l a) p", p=P), tv0)
        vload(vr[16:32, :], I["g_mem"].rearrange("l (a p) -> (l a) p", p=P))
        vload(vr[32:96, :], I["norm_gain_2"].rearrange("l j (a p) -> (l j a) p", p=P))
        vload(vr[96:104, :], I["c_2"].rearrange("l (a p) -> (l a) p", p=P))
        vload(vr[104:106, :], I["gla_head_norm_2"].rearrange("l (a p) -> (l a) p", p=P))
        vload(vr[106:114, :], I["g_final"].rearrange("(a p) -> a p", p=P))
        tvr = vload(vr[114:122, :], I["final_norm_2"].rearrange("(a p) -> a p", p=P))
        COL = dict(g_norm=0, g_mem=16, gain=32, c=96, head=104, g_final=106, f_norm=114)
        ab = [mk_blk(1), mk_blk(1)]
        abv = I["ada_b_2"].rearrange("l (a p) -> (l a) p", p=P)
        tab = [load(sp, f"ab{i}", ab[i].a[0:96, 0:P], abv[96 * i:96 * i + 96, :]) for i in range(2)]
        tx = load(sp, "x", X[:, :, :], I["x"][0].rearrange("(t p) d -> p t d", p=P))
        lamb = mk_blk(2)
        tlam = load(po, "lam", lamb.a, I["diff_lambda"].rearrange("l a b -> (l a b)").unsqueeze(0).to_broadcast([P, 512]))
        ohb = mk_blk(4)
        oh, dmk, rbt = ohb.a[0:32, 0:512], ohb.a[0:20, 512:1024], None
        rbb = mk_blk(3)
        rbt = rbb.a[0:32, 0:20]
        toh = load(po, "oh", oh, C["onehot"])
        tdm = load(po, "dm", dmk, C["dilmask"])
        trb = load(po, "rb", rbt, I["rel_bias"])
        t1 = ve.memset(ones[:, :], 1.0)
        t2 = ve.memset(mhalf[:, :], -0.5)
        tconst = [t1, t2]

        def rstd_of(ss, n, mult, *w):
            ms = smc(n)
            t = ve.ts(ms, ss, mult, EPS, ALU.mult, ALU.add, *w)
            r = smc(n)
            t = po.tt(r, ms, mhalf[:, 0:n], ALU.pow, t, tconst)
            return r, t

        def squares(src, stok):
            jb = mk_blk(8)
            ss = smc(4)
            ts_ = [sc.act(jb.a[:, n * 512:n * 512 + 512], src[:, n // 2, (n % 2) * 512:(n % 2) * 512 + 512],
                          ACT.Square, stok, jb.w, accum=ss[:, n:n + 1]) for n in range(4)]
            jb.release(ts_)
            return ss, ts_

        def rstd2(ss, *w):
            s2 = smc(2)
            sv = ss.rearrange("p (t u) -> p t u", u=2)
            t = ve.tt(s2, sv[:, :, 0], sv[:, :, 1], ALU.add, *w)
            return rstd_of(s2, 2, 1.0 / D, t)

        def diag_rstd(ss, stok):
            r, tr_ = rstd2(ss, stok)
            db = mk_blk(1)
            db.tok = [ve.ts(db.a[:, t * P:t * P + P], ident[:, :], r[:, t:t + 1], None, ALU.mult, None, tr_, tid, db.w)
                      for t in range(2)]
            return db

        mem_norm = diag_rstd(*squares(memb.a.rearrange("p (t d) -> p t d", t=2), [tmem]))

        g = gbank()
        t = pe.tr(GB[g][:, 0:P], vr, ident[:, :], tid, tvr, tv0, inc=True)
        tcols = ve.copy(cols[:, :], GB[g][:, 0:P], t)
        gfree[g] = [tcols]
        vrows.release([t])
        g = gbank()
        for i in range(2):
            t = pe.tr(GB[g][:, 96 * i:96 * i + 96], ab[i].a[0:96, 0:P], ident[0:96, 0:96], tab[i], inc=True)
            ab[i].release([t])
        tadb = ve.copy(adb[:, :], GB[g][:, 0:192], t)
        gfree[g] = [tadb]
        ccol = cols[:, COL["c"]:COL["c"] + 8]
        th = smc(8)
        t = sc.act(th, ccol, ACT.Tanh, tcols, scale=0.5)
        t = ve.stt(th, th, 1.0, ccol, ALU.add, ALU.mult, t)
        tc8 = ve.ts(c8[:, :], th, 0.5, None, ALU.mult, None, t)

        lm = smc(4)
        lprod = lamb.a.rearrange("p (l a b) -> p l a b", l=2, a=4)
        pr = rbb.a[:, 64:320].rearrange("p (l c b) -> p l c b", l=2, c=2)
        t = ve.tt(pr, lprod[:, :, 0::2, :], lprod[:, :, 1::2, :], ALU.mult, tlam)
        t = ve.red(lm, pr.rearrange("p l c b -> p (l c) b"), ALU.add, t)
        t = sc.act(lm, lm, ACT.Exp, t)
        lm2 = lm.rearrange("p (l c) -> p l c", c=2)
        t = ve.tt(nlam[:, :], lm2[:, :, 1], lm2[:, :, 0], ALU.subtract, t)
        lam_init = [0.8 - 0.6 * math.exp(-0.3 * l) for l in range(2)]
        for l in range(2):
            tnlam = ve.ts(nlam[:, l:l + 1], nlam[:, l:l + 1], -lam_init[l], None, ALU.add, None, t)
        lamb.release([t])

        g = gbank()
        t = pe.mm(GB[g][0:20, :], rbt, oh, True, True, toh, trb, inc=True)
        btb = mk_blk(2)
        t2 = ve.tt(btb.a[0:20, :], GB[g][0:20, :], dmk, ALU.add, t, tdm)
        gfree[g] = [t2]
        tbt = t2
        for b in (ohb, rbb):
            b.release([t2, t, tnlam])
        scr = []

        def write_scratch(after):
            scr.append(load(po, "scr", scratch, btb.a[0:20, :].unsqueeze(1).to_broadcast([20, P, 512]), tbt, after))

        for i in range(6):
            sem(f"bias{i}")
        bias_free = [[] for _ in range(6)]
        bias_c = [0] * 6

        def get_bias(sl, i, h):
            r = 3 * sl.j + i
            bias_c[r] += 16
            src = bass.AP(scratch.tensor, h * P * 512 + 127, [[511, P], [1, 384]])
            t = po.dma(bias_t[:, r, :], src, f"bias{r}", bias_c[r], scr[0], bias_free[r])
            return r, t

        def to_T(src, stok, dst, scol=None, bcol=None, const=1.0, ctok=None, nk=8, hn=False, diag=None):
            ready = []
            for b in range(nk // 2):
                g = gbank()
                for i in range(2):
                    for t in range(2):
                        kc = 2 * b + i
                        o = GB[g][:, i * 256 + t * P:i * 256 + t * P + P]
                        if diag is None:
                            tk = pe.tr(o, src[:, t, kc * P:kc * P + P], ident[:, :], stok, gfree[g], tid,
                                       inc=(i == 1 and t == 1))
                        else:
                            tk = pe.mm(o, src[:, t, kc * P:kc * P + P], diag.a[:, t * P:t * P + P], True, True, stok,
                                       gfree[g], diag.tok, inc=(i == 1 and t == 1))
                tmp = None
                if scol is not None:
                    tmp = mk_blk(2)
                    for i in range(2):
                        kc = (2 * b + i) % 2 if hn else 2 * b + i
                        s1 = scol[:, kc:kc + 1]
                        ps = GB[g][:, i * 256:i * 256 + 256]
                        o = tmp.a[:, i * 256:i * 256 + 256]
                        if b % 2:
                            s2 = 0.0 if bcol is None else bcol[:, kc:kc + 1]
                            tv = sc.act(o, ps, ACT.Identity, tk, ctok, tmp.w, bias=s2, scale=s1)
                        elif bcol is None:
                            tv = ve.ts(o, ps, s1, None, ALU.mult, None, tk, ctok, tmp.w)
                        else:
                            tv = ve.ts(o, ps, s1, bcol[:, kc:kc + 1], ALU.mult, ALU.add, tk, ctok, tmp.w)
                    gfree[g] = [tv]
                    tk2 = tv
                ready.append((b, g, tmp, tk if tmp is None else tk2))
                if len(ready) == 2:
                    to_T_split(dst, const, *ready.pop(0))
            to_T_split(dst, const, *ready.pop(0))
            return [tk]

        def to_T_split(dst, const, b, g, tmp, tv):
            hi = dst.hi[:, 2 * b:2 * b + 2, :].rearrange("p a c -> p (a c)")
            lo = dst.lo[:, 2 * b:2 * b + 2, :].rearrange("p a c -> p (a c)")
            fr = dst.waits(2 * b, 2)
            if tmp is None:
                t1 = sc.act(hi, GB[g][:, :], ACT.Copy, tv, fr, scale=const)
                t2 = ve.stt(lo, GB[g][:, :], const, hi.bitcast(F32), ALU.mult, ALU.subtract, t1, fr)
                gfree[g] = [t2]
            else:
                t1 = sc.act(hi, tmp.a, ACT.Copy, tv, fr)
                t2 = ve.tt(lo, tmp.a, hi.bitcast(F32), ALU.subtract, t1, tv, fr)
                tmp.release([t2])
            dst.write(2 * b, 2, [t1, t2])

        def split_ps(dst_hi, dst_lo, src, fr, *w):
            t1 = sc.act(dst_hi, src, ACT.Copy, fr, *w)
            t2 = ve.tt(dst_lo, src, dst_hi.bitcast(F32), ALU.subtract, fr, t1, *w)
            return [t1, t2]

        def exps(S, ap_list, nm, sums, *w):
            for n, a in enumerate(ap_list):
                t = sc.act(a, a, ACT.Exp, *w, bias=nm[:, n:n + 1], accum=sums[:, n:n + 1])
            return t

        def diff_head(l, h, qb, kb, vb, hs):
            def task(sl):
                j = h % 4
                q = qb.a.rearrange("p (m b c) -> p m b c", m=2, b=2)
                k = kb.a.rearrange("p (m b c) -> p m b c", m=2, b=2)
                p0 = 64 * (j % 2)
                vv = vb.a.rearrange("p (t e) -> p t e", t=2)[:, :, j * P:j * P + P]
                r, tb = get_bias(sl, 0, h)
                yield
                for t in range(2):
                    for m in range(2):
                        tk = pe.mm(sl.ps[:, t, m * 256:m * 256 + 256], q[p0:p0 + 64, m, j // 2, t * P:t * P + P],
                                   k[p0:p0 + 64, m, j // 2, :], True, True, qb.tok, kb.tok, sl.ps_free,
                                   inc=(t == 1 and m == 1))
                yield
                S = sl.S[:, 0:1024].rearrange("p (t m k) -> p t m k", t=2, m=2)
                for t in range(2):
                    bt = bias_t[:, r, 128 - 128 * t:384 - 128 * t].unsqueeze(1).to_broadcast([P, 2, 256])
                    tv = ve.stt(S[:, t], sl.ps[:, t, :].rearrange("p (m k) -> p m k", m=2), 0.125, bt,
                                ALU.mult, ALU.add, tk, tb, sl.S_free)
                bias_free[r] = [tv]
                nm, su = smc(4), smc(4)
                S4 = sl.S[:, 0:1024].rearrange("p (n k) -> p n k", n=4)
                tn = ve.red(nm, S4, ALU.max, tv, negate=True)
                te = exps(S4, [S4[:, n, :] for n in range(4)], nm, su, tn, tv)
                yield
                rc = smc(4)
                t1 = ve.recip(rc, su, te)
                r1 = smc(2)
                rc2 = rc.rearrange("p (t m) -> p t m", m=2)
                t1 = ve.ts(r1, rc2[:, :, 1], nlam[:, l:l + 1], None, ALU.mult, None, t1, tnlam)
                for t in range(2):
                    ta = ve.ts(S[:, t, 1, :], S[:, t, 1, :], r1[:, t:t + 1], None, ALU.mult, None, t1, te)
                    ta = ve.stt(S[:, t, 0, :], S[:, t, 0, :], rc[:, 2 * t:2 * t + 1], S[:, t, 1, :],
                                ALU.mult, ALU.add, ta)
                yield
                for kc in range(2):
                    for t in range(2):
                        tk = pe.tr(sl.ps[:, 0, kc * 256 + t * P:kc * 256 + t * P + P],
                                   S[:, t, 0, kc * P:kc * P + P], ident[:, :], ta, inc=(kc == 1 and t == 1))
                sl.S_free = [tk]
                yield
                tw = sc.act(sl.W[:, 0:512], sl.ps[:, 0, :], ACT.Copy, tk, sl.W_free)
                yield
                for t in range(2):
                    for kc in range(2):
                        tk = pe.mm(sl.ps[:, 1, t * P:t * P + P], sl.W[:, kc * 256 + t * P:kc * 256 + t * P + P],
                                   vv[:, kc, :], kc == 0, kc == 1, tw, vb.tok, inc=(kc == 1 and t == 1))
                sl.W_free = [tk]
                yield
                ss = smc(2)
                for t in range(2):
                    t1 = sc.act(sl.W[:, 1024 + t * P:1024 + t * P + P], sl.ps[:, 1, t * P:t * P + P], ACT.Square,
                                tk, accum=ss[:, t:t + 1])
                t2 = ve.copy(vv, sl.ps[:, 1, 0:256].rearrange("p (t e) -> p t e", t=2), tk, t1)
                sl.ps_free = [t2]
                sl.W_free = sl.W_free + [t1]
                rs, tr_ = rstd_of(ss, 2, 1.0 / P, t1)
                yield
                rs2 = smc(2)
                t3 = ve.ts(rs2, rs, 0.5 * (1.0 - lam_init[l]), None, ALU.mult, None, tr_)
                gg = hs["g"].a.rearrange("p (t e) -> p t e", t=2)[:, :, j * P:j * P + P]
                for t in range(2):
                    t4 = ve.stt(vv[:, t, :], vv[:, t, :], rs2[:, t:t + 1], gg[:, t, :], ALU.mult, ALU.mult,
                                t2, t3, hs["g"].tok)
                hs["out"].append(t4)
                hs["n"] += 1
                if hs["n"] == 4:
                    qb.release([t4])
                    kb.release([t4])
            return task

        def dil_head(l, hh, blk, st):
            def task(sl):
                j = hh % 2
                bs = [get_bias(sl, gi, 8 + gi * 4 + hh) for gi in range(3)]
                yield
                for t in range(2):
                    for gi in range(3):
                        o = sl.ps[:, gi // 2, (gi % 2) * 256:(gi % 2) * 256 + 256]
                        tk = pe.mm(o, blk["q"](gi, j)[:, t * P:t * P + P], blk["k"](gi, j), True, True,
                                   blk["qk_tok"](), sl.ps_free, inc=(gi == 2))
                    yield
                    S = sl.S[:, 0:768].rearrange("p (g k) -> p g k", g=3)
                    psf = sl.ps[:, :, :].rearrange("p a b -> p (a b)")
                    for gi in range(3):
                        r, tb = bs[gi]
                        tv = ve.stt(S[:, gi, :], psf[:, gi * 256:gi * 256 + 256], 128 ** -0.5,
                                    bias_t[:, r, 128 - 128 * t:384 - 128 * t], ALU.mult, ALU.add, tk, tb, sl.S_free)
                        if t == 1:
                            bias_free[r] = [tv]
                    nm, su = smc(1), smc(1)
                    tn = ve.red(nm, sl.S[:, 0:768], ALU.max, tv, negate=True)
                    te = sc.act(sl.S[:, 0:768], sl.S[:, 0:768], ACT.Exp, tn, tv, bias=nm, accum=su)
                    yield
                    rc = smc(1)
                    t1 = ve.recip(rc, su, te)
                    t1 = ve.ts(sl.S[:, 0:768], sl.S[:, 0:768], rc, 0.5, ALU.mult, ALU.mult, t1, te)
                    yield
                    for n in range(6):
                        tk = pe.tr(psf[:, n * P:n * P + P], sl.S[:, n * P:n * P + P], ident[:, :], t1, tv,
                                   inc=(n == 5))
                    sl.S_free = [tk]
                    yield
                    W = sl.W[:, :].rearrange("p (n q) -> p n q", n=6)
                    tw = sc.act(W[:, :, t * P:t * P + P], psf[:, 0:768].rearrange("p (n q) -> p n q", n=6),
                                ACT.Copy, tk, sl.W_free)
                    sl.ps_free = [tw]
                for n in range(6):
                    tk = pe.mm(sl.ps[:, 0, 0:256], blk["v"](n // 2, n % 2, j), W[:, n, :], n == 0, n == 5,
                               tw, blk["v_tok"](), inc=(n == 5))
                sl.W_free = [tk]
                yield
                tmp = Blk(1)
                t1 = ve.tt(tmp.a, sl.ps[:, 0, 0:256], blk["g"](j), ALU.mult, tk, blk["g_tok"](), tmp.w)
                sl.ps_free = [t1]
                b = 4 + hh
                OT.write(b, 1, split_ps(OT.hi[:, b, :], OT.lo[:, b, :], tmp.a, OT.waits(b, 1), t1))
                tmp.release(OT.tok[b])
                st["n"] += 1
                if st["n"] == 2:
                    for bb in blk["all"]:
                        bb.release([t1, tk])
            return task

        def mem_head(l, h, B, st):
            def task(sl):
                yield
                q, k, v, gt = B["q"], B["k"], B["v"], B["g"]
                for t in range(2):
                    tk = pe.mm(sl.ps[:, 0, t * 256:t * 256 + 256], q.a[:, h * 256 + t * P:h * 256 + t * P + P],
                               k.a[:, h * 256:h * 256 + 256], True, True, q.tok, k.tok, sl.ps_free, inc=(t == 1))
                yield
                nm, su = smc(2), smc(2)
                p2 = sl.ps[:, 0, :].rearrange("p (t k) -> p t k", t=2)
                S = sl.S[:, 0:512].rearrange("p (t k) -> p t k", t=2)
                tn = ve.red(nm, p2, ALU.max, tk, negate=True)
                nm2 = smc(2)
                tn = ve.ts(nm2, nm, 128 ** -0.5, None, ALU.mult, None, tn)
                for t in range(2):
                    te = sc.act(S[:, t, :], p2[:, t, :], ACT.Exp, tn, sl.S_free, bias=nm2[:, t:t + 1],
                                scale=128 ** -0.5, accum=su[:, t:t + 1])
                yield
                rc = smc(2)
                t1 = ve.recip(rc, su, te)
                for t in range(2):
                    t2 = ve.ts(S[:, t, :], S[:, t, :], rc[:, t:t + 1], 0.5, ALU.mult, ALU.mult, t1, te)
                yield
                for kc in range(2):
                    for t in range(2):
                        tk = pe.tr(sl.ps[:, 1, kc * 256 + t * P:kc * 256 + t * P + P],
                                   S[:, t, kc * P:kc * P + P], ident[:, :], t2, inc=(kc == 1 and t == 1))
                sl.S_free = [tk]
                yield
                tw = sc.act(sl.W[:, 0:512], sl.ps[:, 1, :], ACT.Copy, tk, sl.W_free)
                yield
                for kc in range(2):
                    tk = pe.mm(sl.ps[:, 0, 0:256], v.a[:, kc * 512 + h * P:kc * 512 + h * P + P],
                               sl.W[:, kc * 256:kc * 256 + 256], kc == 0, kc == 1, tw, v.tok, inc=(kc == 1))
                sl.W_free = [tk]
                yield
                tmp = Blk(1)
                t1 = ve.tt(tmp.a, sl.ps[:, 0, 0:256], gt.a[:, h * 256:h * 256 + 256], ALU.mult, tk, gt.tok, tmp.w)
                sl.ps_free = [t1]
                OT.write(h, 1, split_ps(OT.hi[:, h, :], OT.lo[:, h, :], tmp.a, OT.waits(h, 1), t1))
                tmp.release(OT.tok[h])
                st["n"] += 1
                if st["n"] == 4:
                    for bb in (q, k, v, gt):
                        bb.release([t1, tk])
            return task

        def ev_copy(blk, view):
            def f(g, ps, t):
                tc = sc.act(view(g), ps[:, :], ACT.Copy, t, blk.w)
                blk.tok = blk.tok + [tc]
                return [tc]
            return f

        def quad(b, g):
            return b.a[:, g * 512:g * 512 + 512]

        def silu2(dst, ps, t, blk):
            t1 = sc.act(dst, ps, ACT.Tanh, t, blk.w, scale=0.5)
            t2 = ve.stt(dst, dst, 1.0, ps, ALU.add, ALU.mult, t1)
            blk.tok = blk.tok + [t2]
            return [t2]

        xtok = [tx]
        xsq = [None, None]

        def square_of(g, u, xs, tmp, tok, n4):
            return sc.act(tmp, xs, ACT.Square, tok, accum=n4[:, 2 * g + u:2 * g + u + 1])

        mkvb = []
        mdiag = []

        def mem_kv(l, mb, tm):
            if l == 0:
                mv = mb.a.rearrange("p (t d) -> p t d", t=2)
                mdiag.append(mem_norm)
            else:
                mv = mb
            gm = cols[:, COL["g_mem"] + 8 * l:COL["g_mem"] + 8 * l + 8]
            rel = to_T(mv, tm, OT, scol=gm, ctok=tcols, diag=mdiag[0])
            if l == 0:
                mb.release(rel)
            else:
                for b in mb.b + mdiag:
                    b.release(rel)
            B = {"k": mk_blk(4)}
            tg = gemm(OT, 0, ("mkv", l, 0), D, "FF", ev_copy(B["k"], lambda g: quad(B["k"], g)))
            if l == 0:
                write_scratch(tg)
            B["v"] = mk_blk(4)
            gemm(OT, 0, ("mkv", l, 1), D, "TT", ev_copy(B["v"], lambda g: quad(B["v"], g)))
            mkvb.append(B)

        def layer1(l):
            if l == 0:
                mem_kv(0, memb, [tmem])
                xsq[:] = squares(X, [tx])
            B = mkvb.pop(0)
            db = diag_rstd(*xsq)
            gn = cols[:, COL["g_norm"] + 8 * l:COL["g_norm"] + 8 * l + 8]
            db.release(to_T(X, xtok, HT, scol=gn, ctok=tcols, diag=db))
            B["q"], B["g"] = mk_blk(4), mk_blk(4)
            gemm(HT, 0, ("mq", l), D, "FF", ev_copy(B["q"], lambda g: quad(B["q"], g)))
            if l == 0:
                btb.release(scr)
            gemm(HT, 0, ("mg", l), D, "FF", lambda g, ps, t: silu2(quad(B["g"], g), ps[:, :], t, B["g"]))
            st = {"n": 0}
            for h in range(4):
                pend.append(mem_head(l, h, B, st))
            sts = [st]
            for pr in range(2):
                b1 = mk_blk(4)
                gemm(HT, 0, ("dil", l, pr, 0), D, "FF", ev_copy(b1, lambda g: quad(b1, g)))
                b2 = mk_blk(4)
                gemm(HT, 0, ("dil", l, pr, 1), D, "FF", ev_copy(b2, lambda g: quad(b2, g)))
                b3 = mk_blk(4)
                gemm(HT, 0, ("dil", l, pr, 2), D, "FF", ev_copy(b3, lambda g: quad(b3, g)))
                b4 = mk_blk(4)
                gemm(HT, 0, ("dil", l, pr, 3), D, "TT", ev_copy(b4, lambda g: quad(b4, g)))
                b5 = mk_blk(4)

                def ev(g, ps, t, b5=b5):
                    if g == 0:
                        tc = sc.act(quad(b5, 0), ps[:, :], ACT.Copy, t, b5.w)
                        b5.tok = b5.tok + [tc]
                        return [tc]
                    return silu2(quad(b5, 1), ps[:, :], t, b5)
                gemm(HT, 0, ("dil", l, pr, 4), D, "TF", ev)

                def bl(b, n):
                    return b.a[:, n * 256:n * 256 + 256]

                def vv(gi, kc, j, b4=b4, b5=b5):
                    if gi < 2:
                        return b4.a[:, kc * 512 + gi * 256 + j * P:kc * 512 + gi * 256 + j * P + P]
                    return b5.a[:, kc * 256 + j * P:kc * 256 + j * P + P]
                blk = {"q": lambda gi, j, b1=b1, b2=b2: bl(b1, gi * 2 + j) if gi < 2 else bl(b2, j),
                       "k": lambda gi, j, b2=b2, b3=b3: bl(b3, gi * 2 + j) if gi < 2 else bl(b2, 2 + j),
                       "v": vv, "g": lambda j, b5=b5: bl(b5, 2 + j),
                       "qk_tok": lambda b1=b1, b2=b2, b3=b3: b1.tok + b2.tok + b3.tok,
                       "v_tok": lambda b4=b4, b5=b5: b4.tok + b5.tok, "g_tok": lambda b5=b5: b5.tok,
                       "all": [b1, b2, b3, b4, b5]}
                st2 = {"n": 0}
                sts.append(st2)
                for hh in (2 * pr, 2 * pr + 1):
                    pend.append(dil_head(l, hh, blk, st2))
            merged = mk_blk(8)
            mg = merged.a.rearrange("p (t d) -> p t d", t=2)
            mtok = {}

            def gate_of(i, u):
                gb = mk_blk(4)

                def ev(g, ps, t):
                    tc = sc.act(quad(gb, g), ps[:, :], ACT.Tanh, t, gb.w, scale=0.5)
                    gb.tok = gb.tok + [tc]
                    return [tc]
                gemm(HT, 0, ("gate", l, i, u), D, "TT", ev)
                return gb

            def y_of(key, A, b0, K, u, gb, first):
                last = []

                def ev(g, ps, t):
                    m = mg[:, g, u * 512:u * 512 + 512]
                    if first:
                        tv = ve.stt(m, quad(gb, g), 1.0, ps[:, :], ALU.add, ALU.mult, t, gb.tok, merged.w)
                        mtok[(g, u)] = tv
                    else:
                        tv = ve.stt(quad(gb, g), quad(gb, g), 1.0, ps[:, :], ALU.add, ALU.mult, t, gb.tok)
                        mtok[(g, u)] = po.tt(m, m, quad(gb, g), ALU.add, tv, mtok[(g, u)])
                    last.append(tv)
                    last.append(mtok[(g, u)])
                    return [tv]
                gemm(A, b0, key, K, "TT", ev)
                gb.release(last)

            for u in range(2):
                gb = gate_of(2, u)
                drain(lambda: sts[0]["n"] == 4)
                y_of(("ym", l, u), OT, 0, 512, u, gb, True)
            V = []
            for hf in range(2):
                qb = mk_blk(4)
                gemm(HT, 0, ("diff", l, hf, 0), D, "FF", ev_copy(qb, lambda g: quad(qb, g)))
                kb = mk_blk(4)
                gemm(HT, 0, ("diff", l, hf, 1), D, "FF", ev_copy(kb, lambda g: quad(kb, g)))
                vb = mk_blk(4)
                gemm(HT, 0, ("diff", l, hf, 2), D, "TT", ev_copy(vb, lambda g: quad(vb, g)))
                gb = mk_blk(4)
                hs = {"g": gb, "out": [], "n": 0}
                gemm(HT, 0, ("diff", l, hf, 3), D, "TT",
                     lambda g, ps, t, gb=gb: silu2(quad(gb, g), ps[:, :], t, gb))
                for h in range(4 * hf, 4 * hf + 4):
                    pend.append(diff_head(l, h, qb, kb, vb, hs))
                V.append((vb, gb, hs))
            drain(lambda: all(s["n"] == 2 for s in sts[1:]))
            for u in range(2):
                gb = gate_of(1, u)
                if u == 1 and l == 0:
                    mb = Tiles([mk_blk(4), mk_blk(4)])
                    tm = [load(po, f"mem1{t}", mb.b[t].a, I["mem"][0][t * P:t * P + P, :], mb.b[t].w)
                          for t in range(2)]
                y_of(("yb", l, u), OT, 4, 512, u, gb, False)
            if l == 0:
                mem_kv(1, mb, tm)
            gbs = [gate_of(0, u) for u in range(2)]
            drain(lambda: not busy())
            for hf in range(2):
                vb, gb, hs = V[hf]
                src = vb.a.rearrange("p (t e) -> p t e", t=2)
                sub = Sub(OT, 4 * hf)
                rel = to_T(src, hs["out"], sub, nk=4)
                vb.release(rel)
                gb.release(hs["out"])
            for u in range(2):
                y_of(("ya", l, u), OT, 0, D, u, gbs[u], False)
            rel = to_T(mg, list(mtok.values()), HT, const=0.5)
            merged.release(rel)
            nx, sq, n4 = [], [], smc(4)
            for u in range(2):
                def ev(g, ps, t):
                    tmp = mk_blk(2)
                    xs = X[:, g, u * 512:u * 512 + 512]
                    tv = ve.tt(xs, ps[:, :], xs, ALU.add, t, xtok)
                    nx.append(tv)
                    sq.append(square_of(g, u, xs, tmp.a, [tv] + tmp.w, n4))
                    tmp.release(sq[-1:])
                    return [tv]
                gemm(HT, 0, ("wo", l, u), D, "TT", ev, last=(u == 1))
            xtok[:] = nx + sq
            xsq[:] = [n4, sq]

        class Tiles:

            def __init__(self, b):
                self.b = b

            def __getitem__(self, at):
                return self.b[at[1]].a[:, at[2]]

        class Sub:

            def __init__(self, A, b0):
                self.A, self.b0 = A, b0
                self.hi, self.lo = A.hi[:, b0:8, :], A.lo[:, b0:8, :]

            def write(self, b, n, t):
                self.A.write(self.b0 + b, n, t)

            def waits(self, b, n):
                return self.A.waits(self.b0 + b, n)

        def bcast(c0, src, stok):
            b = mk_blk(4)
            for hf in range(2):
                g = gbank()
                for n in range(4):
                    c = c0 + hf * 4 + n
                    t = pe.mm(GB[g][:, n * P:n * P + P], src[:, c:c + 1].to_broadcast([P, P]), ident[:, :], True, True,
                              stok, gfree[g], inc=(n == 3))
                tv = sc.act(b.a[:, hf * 512:hf * 512 + 512], GB[g][:, :], ACT.Copy, t, b.w)
                gfree[g] = [tv]
                b.tok = b.tok + [tv]
            return b

        def final_norm(c0, dst):
            gb = bcast(c0, cols, tcols)
            r, tr_ = rstd2(xsq[0], xsq[1])
            ts_ = [ve.stt(dst[:, t, :], X[:, t, :], r[:, t:t + 1], gb.a, ALU.mult, ALU.mult, tr_, xtok, gb.tok)
                   for t in range(2)]
            gb.release(ts_)
            return ts_

        def modulated(l, jn):
            m = mod[:, l * 48 + jn * 24:l * 48 + jn * 24 + 24]
            gain = cols[:, COL["gain"] + 16 * l + 8 * jn:COL["gain"] + 16 * l + 8 * jn + 8]
            a = smc(8)
            ta = ve.stt(a, m[:, 8:16], 1.0, gain, ALU.add, ALU.mult, mod_tok[l], tcols)
            db = diag_rstd(*xsq)
            db.release(to_T(X, xtok, HT, scol=a, bcol=m[:, 0:8], ctok=[ta, mod_tok[l]], diag=db))

        def residual(gb, u, nx, sq, n4):
            def ev(g, ps, t):
                tmp = mk_blk(2)
                xs = X[:, g, u * 512:u * 512 + 512]
                t1 = ve.tt(tmp.a, ps[:, :], gb.a[:, u * 512:u * 512 + 512], ALU.mult, t, gb.tok, tmp.w)
                t2 = ve.tt(xs, xs, tmp.a, ALU.add, t1, xtok)
                nx.append(t2)
                sq.append(square_of(g, u, xs, tmp.a, t2, n4))
                tmp.release(sq[-1:])
                return [t1]
            return ev

        def softmax_pv2(sl, t, S3, wd, tv, tn, nm, pv, ob, hp):
            nk = t + 1
            K = nk * P
            su = smc(2)
            te = exps(None, [S3[:, n, 0:wd] for n in range(2)], nm, su, tn, tv)
            yield
            rc = smc(2)
            t1 = ve.recip(rc, su, te)
            for n in range(2):
                t2 = ve.ts(S3[:, n, 0:K], S3[:, n, 0:K], rc[:, n:n + 1], None, ALU.mult, None, t1, te)
            yield
            for kc in range(nk):
                for n in range(2):
                    tk = pe.tr(sl.ps[:, (kc * 2 + n) * P:(kc * 2 + n) * P + P], S3[:, n, kc * P:kc * P + P],
                               ident[:, :], t2, inc=(kc == nk - 1 and n == 1))
            sl.S_free = [tk]
            yield
            tw = sc.act(sl.W[:, 0:2 * K], sl.ps[:, 0:2 * K], ACT.Copy, tk, sl.W_free)
            yield
            W = sl.W.rearrange("p (k n q) -> p k n q", k=2, n=2)
            r0 = 64 * hp
            tk = pv(sl.ps[r0:r0 + 64, 0:256].rearrange("p (n q) -> p n q", n=2), W, nk, tw)
            sl.W_free = [tk]
            yield
            tt_ = split_ps(OT.hi[r0:r0 + 64, ob:ob + 2, t * P:t * P + P], OT.lo[r0:r0 + 64, ob:ob + 2, t * P:t * P + P],
                           sl.ps[r0:r0 + 64, 0:256].rearrange("p (n q) -> p n q", n=2), OT.waits(ob, 2), tk)
            for b in (ob, ob + 1):
                OT.tok[b] = OT.tok[b] + tt_
            sl.ps_free = [tt_[-1]]

        def swa_layer(l):
            j = l // 3
            cb = mk_blk(3)
            rp = cb.a[:, 0:256].rearrange("p (s t d) -> p s t d", s=2, t=2)
            msk = cb.a[:, 256:512]
            snk = cb.a[:, 512:528]
            trp = load(po, f"rp{l}", cb.a[:, 0:256], C["rope"], cb.w)
            tms = load(po, f"ms{l}", msk, C["swamask"], cb.w)
            tsk = load(po, f"sk{l}", snk, I["swa_sinks_2"][j].unsqueeze(0).to_broadcast([P, 16]), cb.w)
            modulated(l, 0)

            def rope_bank(ps, t, dst, nh, tb, blk):
                tmp = Blk(2)
                x = ps[:, 0:nh * 64].rearrange("p (h a b) -> p h a b", a=2, b=32)
                d = dst[:, 0:nh * 64].rearrange("p (h a b) -> p h a b", a=2, b=32)
                m = tmp.a[:, 0:nh * 64].rearrange("p (h a b) -> p h a b", a=2, b=32)
                c = rp[:, 0, t, :].rearrange("p (a b) -> p a b", a=2).unsqueeze(1).to_broadcast([P, nh, 2, 32])
                s = rp[:, 1, t, :].rearrange("p (a b) -> p a b", a=2).unsqueeze(1).to_broadcast([P, nh, 2, 32])
                t1 = ve.tt(d, x, c, ALU.mult, tb, trp, blk.w)
                t2 = ve.tt(m, x[:, :, ::-1, :], s, ALU.mult, tb, trp, tmp.w)
                t3 = po.tt(dst[:, 0:nh * 64], dst[:, 0:nh * 64], tmp.a[:, 0:nh * 64], ALU.add, t1, t2)
                tmp.release([t3])
                return t2, t3

            kvb = mk_blk(4)

            def ev_kv(g, ps, t):
                t2, t3 = rope_bank(ps, g, kvb.a[:, g * 512:g * 512 + 256], 4, t, kvb)
                t4 = sc.act(kvb.a[:, g * 512 + 256:g * 512 + 512], ps[:, 256:512], ACT.Copy, t, t2, kvb.w)
                kvb.tok = kvb.tok + [t3, t4]
                return [t4]
            gemm(HT, 0, ("swa", l, 2), D, "TT", ev_kv)
            gb = bcast(l * 48 + 16, mod, mod_tok[l])
            kT = mk_blk(4)
            kt = kT.a.rearrange("p (n c) -> p n c", n=4)

            def kv_T():
                for n2 in range(2):
                    g = gbank()
                    for n in (2 * n2, 2 * n2 + 1):
                        for t in range(2):
                            for dup in range(2):
                                c = (n % 2) * 256 + t * P
                                tk = pe.mm(GB[g][64 * dup:64 * dup + 64, c:c + P],
                                           kvb.a[:, t * 512 + n * 64:t * 512 + n * 64 + 64], ident[:, :], True, True,
                                           kvb.tok, gfree[g], inc=(n % 2 == 1 and t == 1 and dup == 1), skip=True)
                    tc = sc.act(kT.a[:, n2 * 512:n2 * 512 + 512], GB[g][:, :], ACT.Copy, tk, kT.w)
                    gfree[g] = [tc]
                    kT.tok = kT.tok + [tc]
            deferred.append(kv_T)
            st = {"n": 0, "t": []}
            qTs = []
            halve()
            for b in range(8):
                OT.tok[b] = []

            def heads(kv, hp, t, qT):
                def task(sl):
                    q = qT.a.rearrange("p (n c) -> p n c", n=4)
                    K = (t + 1) * P
                    wd = K + 1
                    p0 = 64 * hp
                    for n in range(2):
                        tk = pe.mm(sl.ps[:, n * 256:n * 256 + K], q[p0:p0 + 64, (2 * kv + n) % 4, t * P:t * P + P],
                                   kt[p0:p0 + 64, kv, 0:K], True, True, qT.tok, kT.tok, sl.ps_free, inc=(n == 1))
                    yield
                    S3 = sl.S[:, 0:514].rearrange("p (n k) -> p n k", n=2)
                    mk = msk[:, 256 - K:256].unsqueeze(1).to_broadcast([P, 2, K])
                    t1 = ve.stt(S3[:, :, 0:K], sl.ps.rearrange("p (n k) -> p n k", n=2)[:, :, 0:K], 0.125, mk,
                                ALU.mult, ALU.add, tk, tms, sl.S_free)
                    t2 = ve.copy(S3[:, :, K], snk[:, 4 * kv + hp:4 * kv + hp + 3:2], tsk, sl.S_free)
                    nm = smc(2)
                    tn = ve.red(nm, S3[:, :, 0:wd], ALU.max, t1, t2, negate=True)

                    def pv(o, W, nk, tw):
                        for kc in range(nk):
                            v = kvb.a[:, kc * 512 + 256 + kv * 64:kc * 512 + 256 + kv * 64 + 64]
                            tk = pe.mm(o, v, W[:, kc], kc == 0, kc == nk - 1, tw, kvb.tok, inc=(kc == nk - 1),
                                       skip=True)
                        return tk
                    yield from softmax_pv2(sl, t, S3, wd, t1, tn, nm, pv, 2 * kv, hp)
                    st["n"] += 1
                    st["t"] += [sl.ps_free[0]]
                return task

            for u in range(2):
                qt = mk_blk(4)

                def ev_q(g, ps, t):
                    t2, t3 = rope_bank(ps, g, qt.a[:, g * 512:g * 512 + 512], 8, t, qt)
                    qt.tok = qt.tok + [t3]
                    return [t2]
                gemm(HT, 0, ("swa", l, u), D, "TT", ev_q)

                def q_T(u=u, qt=qt):
                    qT = mk_blk(4)
                    for n2 in range(2):
                        g = gbank()
                        for n in range(2):
                            for t in range(2):
                                c = t * 512 + (n2 * 2 + n) * P
                                tk = pe.tr(GB[g][:, n * 256 + t * P:n * 256 + t * P + P], qt.a[:, c:c + P],
                                           ident[:, :], qt.tok, gfree[g], inc=(n == 1 and t == 1))
                        tc = sc.act(qT.a[:, n2 * 512:n2 * 512 + 512], GB[g][:, :], ACT.Copy, tk, qT.w)
                        gfree[g] = [tc]
                        qT.tok = qT.tok + [tc]
                    qt.release([tk])
                    qTs.append(qT)
                    for kv in (2 * u, 2 * u + 1):
                        for t in range(2):
                            for hp in range(2):
                                pend.append(heads(kv, hp, t, qT))
                deferred.append(q_T)
            step()
            deferred.pop()()
            widen(4)
            drain(lambda: not busy())
            whole()
            for b in qTs + [kT, kvb, cb]:
                b.release(st["t"])
            return gb

        def logsig(z, n, ztok, tmp):
            t = ve.stt(tmp, z, -1.0, z, ALU.mult, ALU.max, ztok)
            t = sc.act(tmp, tmp, ACT.Exp, t, scale=-1.0)
            t = sc.act(tmp, tmp, ACT.Ln, t, bias=1.0)
            return ve.stt(z, z, 0.0, tmp, ALU.min, ALU.subtract, t)

        def narrow(w, name):
            wb = mk_blk(1)
            src = wb.a[:, 0:P].rearrange("p (c n) -> p c n", n=16)
            tl = load(po, name, src, w.rearrange("(c p) n -> p c n", p=P), wb.w)
            t1 = sc.act(w16h[:, :, :], src, ACT.Copy, tl, w16_free)
            t2 = ve.tt(w16l[:, :, :], src, w16h[:, :, :].bitcast(F32), ALU.subtract, t1, w16_free)
            wb.release([t2])
            g = gbank()
            o = GB[g][0:16, 0:256]
            for kc in range(8):
                pe.wait(t1, t2, HT.tok[kc], gfree[g])
                pe.mm(o, w16h[:, kc, :], HT.hi[:, kc, :], kc == 0, False, skip=True)
                pe.mm(o, w16l[:, kc, :], HT.hi[:, kc, :], False, False, skip=True)
                tk = pe.mm(o, w16h[:, kc, :], HT.lo[:, kc, :], False, kc == 7, skip=True, inc=(kc == 7))
            w16_free[:] = [tk]
            return g, tk

        w16_free = []

        def gla_layer(l):
            modulated(l, 0)
            dec, mk = mk_blk(5), mk_blk(4)
            td = load(po, "gd", dec.a[:, 0:1152], C["gladec"], dec.w)
            tmk = load(po, "gm", mk.a, C["glamask"], mk.w)
            qT, kT = mk_blk(4), mk_blk(4)
            gemm(HT, 0, ("gla", l, 0), D, "FF", ev_copy(qT, lambda g: quad(qT, g)))
            gemm(HT, 0, ("gla", l, 1), D, "FF", ev_copy(kT, lambda g: quad(kT, g)))
            g, tk = narrow(I["gla_w_in_2"][0][:, 3072:3088], "w16a")
            aT = mk_blk(1)
            ta = ve.copy(aT.a[0:16, :], GB[g][0:16, 0:256], tk, aT.w)
            gfree[g] = [ta]
            wg, bgt = mk_blk(2), mk_blk(2)
            tw = load(po, "wgu", wg.a[0:16, :], I["gla_w_gate_up_2"][0], wg.w)
            tb = load(po, "bgt", bgt.a, I["gla_b_gate_2"].to_broadcast([P, 512]), bgt.w)
            la = mk_blk(4)
            tl = []
            tmp = mk_blk(2)
            for t in range(2):
                g = gbank()
                tk = pe.mm(GB[g][:, :], aT.a[0:16, t * P:t * P + P], wg.a[0:16, :], True, True, ta, tw, gfree[g],
                           inc=True)
                z = la.a[:, t * 512:t * 512 + 512]
                t1 = ve.tt(z, GB[g][:, :], bgt.a, ALU.add, tk, tb, la.w, tmp.w)
                gfree[g] = [t1]
                tl.append(logsig(z, 512, t1, tmp.a))
                tmp.w = [tl[-1]]
            for b in (aT, wg, bgt, tmp):
                b.release([tl[-1], tk])
            la.tok = tl
            gb = bcast(l * 48 + 16, mod, mod_tok[l])
            st = {"n": 0, "t": []}
            V, R = [mk_blk(4), mk_blk(4)], [mk_blk(4), mk_blk(4)]

            def head(h):
                def task(sl):
                    q = qT.a[:, h * 256:h * 256 + 256]
                    k = kT.a[:, h * 256:h * 256 + 256]
                    psf = sl.ps[:, :, :].rearrange("p a b -> p (a b)")
                    ps8 = psf.rearrange("p (n c) -> p n c", n=8)
                    S8 = sl.S[:, 0:1024].rearrange("p (n c) -> p n c", n=8)
                    E = sl.S[:, 0:1024]
                    W = sl.W
                    kc0 = W[:, 1280:1536]
                    for t in range(2):
                        yield
                        for hf in range(2):
                            if hf == 0:
                                tk = pe.mm(sl.ps[:, 0, :], la.a[:, t * 512 + h * P:t * 512 + h * P + P],
                                           dec.a[:, 0:512], True, True, la.tok, td, sl.ps_free)
                            else:
                                pe.mm(sl.ps[:, 1, 0:384], la.a[:, t * 512 + h * P:t * 512 + h * P + P],
                                      dec.a[:, 512:896], True, True)
                                tk = pe.mm(sl.ps[:, 1, 384:512], la.a[:, t * 512 + h * P:t * 512 + h * P + P],
                                           dec.a[:, 896 + 128 * t:1024 + 128 * t], True, True, inc=True)
                        yield
                        te = sc.act(E, psf, ACT.Exp, tk, sl.S_free)
                        yield
                        qt = q[:, t * P:t * P + P]
                        kt = k[:, t * P:t * P + P]
                        KE = W[:, 0:1024].rearrange("p (n c) -> p n c", n=8)
                        t1 = po.tt(KE, S8, kt.unsqueeze(1).to_broadcast([P, 8, P]), ALU.mult, te, kT.tok, sl.W_free)
                        if t == 0:
                            t3 = po.copy(kc0[:, 0:P], KE[:, 7, :], t1)
                        t2 = ve.tt(S8, S8, qt.unsqueeze(1).to_broadcast([P, 8, P]), ALU.mult, te, t1, qT.tok)
                        yield
                        if t == 1:
                            tx_ = pe.mm(psf[:, 0:P], kc0[:, 0:P], S8[:, 7, :], True, True, t2, t3, inc=True)
                            tw01 = sc.act(kc0[:, P:2 * P], psf[:, 0:P], ACT.Copy, tx_, scale=128 ** -0.5)
                        for n in range(8):
                            lh, rh = (KE[:, n, :], S8[:, n, :]) if n < 7 else (kt, qt)
                            tk = pe.mm(ps8[:, n, :], lh, rh, True, True, t1, t2, tw01 if t == 1 else None,
                                       inc=(n == 7))
                        yield
                        tm = ve.tt(E, psf, mk.a, ALU.mult, tk, tmk)
                        tr_ = ve.red(W[:, 1024 + t * P:1024 + t * P + P], S8.rearrange("p n c -> p c n"), ALU.add, tm,
                                     sl.W_free)
                        sl.ps_free = [tm]
                        sl.S_free = [tr_]
                        sl.W_free = [tk, t3]
                    wt = [t1, tr_, tw01]
                    yield
                    vb = V[h // 2]

                    def v(t):
                        return vb.a[:, t * 512 + (h % 2) * 256:t * 512 + (h % 2) * 256 + 256]
                    while len(vb.tok) < 2:
                        yield
                    pe.mm(psf[:, 0:256], W[:, 1024:1152], v(0), True, True, wt, vb.tok, sl.ps_free)
                    pe.mm(psf[:, 256:512], kc0[:, P:2 * P], v(0), True, False)
                    tk = pe.mm(psf[:, 256:512], W[:, 1152:1280], v(1), False, True, inc=True)
                    yield
                    ss = smc(2)
                    for t in range(2):
                        t1 = sc.act(E[:, t * 256:t * 256 + 256], psf[:, t * 256:t * 256 + 256], ACT.Square, tk, sl.S_free,
                                    accum=ss[:, t:t + 1])
                    rs, tr_ = rstd_of(ss, 2, 1.0 / 256, t1)
                    rs2 = smc(2)
                    t3 = ve.ts(rs2, rs, 0.5, None, ALU.mult, None, tr_)
                    yield
                    rb = R[h // 2]
                    while len(rb.tok) < 2:
                        yield
                    for t in range(2):
                        ra = rb.a[:, t * 512 + (h % 2) * 256:t * 512 + (h % 2) * 256 + 256]
                        t4 = ve.stt(ra, psf[:, t * 256:t * 256 + 256], rs2[:, t:t + 1], ra, ALU.mult, ALU.mult,
                                    t3, t1, rb.tok)
                    sl.ps_free = [t4]
                    sl.W_free = [tk]
                    sl.S_free = [t1]
                    st["n"] += 1
                    st["t"].append(t4)
                return task

            for h in range(2):
                pend.append(head(h))
            gemm(HT, 0, ("gla", l, 2), D, "TT", ev_copy(V[0], lambda g: quad(V[0], g)))
            gemm(HT, 0, ("gla", l, 3), D, "TT", ev_copy(V[1], lambda g: quad(V[1], g)))
            gemm(HT, 0, ("gla", l, 4), D, "TT", lambda g, ps, t: silu2(quad(R[0], g), ps[:, :], t, R[0]))
            gemm(HT, 0, ("gla", l, 5), D, "TT", lambda g, ps, t: silu2(quad(R[1], g), ps[:, :], t, R[1]))
            for h in range(2, 4):
                pend.append(head(h))
            drain(lambda: not busy())
            for b in V + [qT, kT, la, dec, mk]:
                b.release(st["t"])
            hn = cols[:, COL["head"]:COL["head"] + 2]
            for i in range(2):
                rel = to_T(R[i].a.rearrange("p (t e) -> p t e", t=2), st["t"], Sub(OT, 4 * i), scol=hn, ctok=tcols,
                           nk=4, hn=True)
                R[i].release(rel)
            return gb

        def fox_layer(l):
            modulated(l, 0)
            st = {"n": 0, "t": []}
            rel_list = []
            qb, kb = mk_blk(4), mk_blk(4)
            gemm(HT, 0, ("fox", l, 0), D, "FF", ev_copy(qb, lambda g: quad(qb, g)))
            gemm(HT, 0, ("fox", l, 2), D, "FF", ev_copy(kb, lambda g: quad(kb, g)))
            g, tk = narrow(I["fox_w_in_2"][0][:, 3072:3088], "w16b")
            fb = mk_blk(1)
            z, bf, tp = fb.a[:, 0:32], fb.a[:, 32:64], fb.a[:, 64:96]
            cb = mk_blk(3)
            cum, msk = cb.a[:, 0:512], cb.a[:, 512:768]
            tcm = load(po, "cum", cum, C["cum"], cb.w)
            tmk = load(po, "fm", msk, C["foxmask"], cb.w)
            tbf = load(po, "bf", bf[:, 0:16], I["fox_b_f_2"].to_broadcast([P, 16]), fb.w)
            zt = mk_blk(1)
            tc = ve.copy(zt.a[0:16, :], GB[g][0:16, 0:256], tk, zt.w)
            gfree[g] = [tc]
            g = gbank()
            for t in range(2):
                tk = pe.tr(GB[g][:, t * 16:t * 16 + 16], zt.a[0:16, t * P:t * P + P], ident[0:16, 0:16], tc, gfree[g],
                           inc=(t == 1))
            zt.release([tk])
            for t in range(2):
                t1 = ve.tt(z[:, t * 16:t * 16 + 16], GB[g][:, t * 16:t * 16 + 16], bf[:, 0:16], ALU.add, tk, tbf, fb.w)
            gfree[g] = [t1]
            tz = logsig(z, 32, t1, tp)
            lq = fb.a[:, 96:128]
            g = gbank()
            for t in range(2):
                for jj in range(t + 1):
                    tk = pe.mm(GB[g][:, t * 16:t * 16 + 16], cum[:, jj * 256 + t * P:jj * 256 + t * P + P],
                               z[:, jj * 16:jj * 16 + 16], jj == 0, jj == t, tz, tcm, gfree[g],
                               inc=(t == 1 and jj == t))
            tlq = ve.copy(lq, GB[g][:, 0:32], tk)
            gfree[g] = [tlq]
            z8 = fb.a[:, 128:160]
            tz8 = ve.ts(z8, z, -8.0, None, ALU.mult, None, tz)
            gb = bcast(l * 48 + 16, mod, mod_tok[l])
            for b in range(8):
                OT.tok[b] = []

            def heads(h0, hp, t, qb, kb, vb):
                def task(sl):
                    K = (t + 1) * P
                    p0 = 64 * hp
                    for n in range(2):
                        h = h0 + 2 * n + hp
                        bl = (h // 2) % 4
                        o = sl.ps[:, n * 256:n * 256 + K]
                        pe.mm(o, qb.a[p0:p0 + 64, bl * 256 + t * P:bl * 256 + t * P + P],
                              kb.a[p0:p0 + 64, bl * 256:bl * 256 + K], True, False, qb.tok, kb.tok, tz8, tcm,
                              sl.ps_free, skip=True)
                        for jj in range(t + 1):
                            k0 = jj * P
                            tk = pe.mm(sl.ps[:, n * 256 + k0:n * 256 + K],
                                       z8[:, jj * 16 + h:jj * 16 + h + 1].to_broadcast([P, P]),
                                       cum[:, jj * 256 + k0:jj * 256 + K], False, jj == t, inc=(n == 1 and jj == t),
                                       skip=True)
                    yield
                    S3 = sl.S[:, 0:514].rearrange("p (n k) -> p n k", n=2)
                    for n in range(2):
                        h = h0 + 2 * n + hp
                        t1 = ve.ts(S3[:, n, 0:K], sl.ps[:, n * 256:n * 256 + K], 0.125,
                                   lq[:, t * 16 + h:t * 16 + h + 1], ALU.mult, ALU.add, tk, tlq, sl.S_free)
                    t2 = ve.tt(S3[:, :, 0:K], S3[:, :, 0:K], msk[:, 256 - K:256].unsqueeze(1).to_broadcast([P, 2, K]),
                               ALU.add, t1, tmk)
                    nm = smc(2)
                    tn = ve.red(nm, S3[:, :, 0:K], ALU.max, t2, negate=True)

                    def pv(o, W, nk, tw):
                        for n in range(2):
                            h = (h0 + 2 * n + hp) % 8
                            for kc in range(nk):
                                tk = pe.mm(o[:, n], vb.a[:, kc * 512 + h * 64:kc * 512 + h * 64 + 64], W[:, kc, n, :],
                                           kc == 0, kc == nk - 1, tw, vb.tok, inc=(n == 1 and kc == nk - 1),
                                           skip=True)
                        return tk
                    yield from softmax_pv2(sl, t, S3, K, t2, tn, nm, pv, h0 // 2, hp)
                    st["n"] += 1
                    st["t"] += [sl.ps_free[0]]
                return task

            halve()
            for u in range(2):
                if u:
                    qb, kb = mk_blk(4), mk_blk(4)
                    gemm(HT, 0, ("fox", l, u), D, "FF", ev_copy(qb, lambda g: quad(qb, g)))
                    gemm(HT, 0, ("fox", l, 2 + u), D, "FF", ev_copy(kb, lambda g: quad(kb, g)))
                vb = mk_blk(4)
                gemm(HT, 0, ("fox", l, 4 + u), D, "TT", ev_copy(vb, lambda g: quad(vb, g)))
                rel_list += [qb, kb, vb]
                for h0 in (8 * u, 8 * u + 4):
                    for t in range(2):
                        for hp in range(2):
                            pend.append(heads(h0, hp, t, qb, kb, vb))
            widen(2)
            drain(lambda: not busy())
            whole()
            for b in rel_list + [fb, cb]:
                b.release(st["t"])
            return gb

        def ffn(l):
            modulated(l, 1)
            dacc_wait = [slots[0].ps_free + slots[1].ps_free]

            def down(v):
                b0 = 2 * (v % 4)
                for kc in range(2):
                    s, wt = take(("dn", l, v))
                    pe.wait(wt, OT.tok[b0 + kc])
                    if v == 0 and kc == 0:
                        pe.wait(dacc_wait[0])
                    for t in range(2):
                        a = (OT.hi[:, b0 + kc, t * P:t * P + P], OT.lo[:, b0 + kc, t * P:t * P + P])
                        for n in range(2):
                            o = AB[t][:, n, :]
                            pe.mm(o, a[0], whi[:, s, n, :], v == 0 and kc == 0, False, skip=True)
                            pe.mm(o, a[0], wlo[:, s, n, :], False, False, skip=True)
                            tk = pe.mm(o, a[1], whi[:, s, n, :], False, False, skip=True,
                                       inc=(t == 1 and n == 1))
                    spl_free[s] = [tk]
                    OT.free[b0 + kc] = [tk]
                return tk

            for v in range(12):
                if v < 11:
                    b0 = 2 * (v % 4)
                    tmp = mk_blk(4)
                    t1_, t2_ = tmp.a[:, 0:512], tmp.a[:, 512:1024]
                    keep = {}

                    def ev(g, ps, t):
                        if g == 0:
                            ta = sc.act(t1_, ps[:, :], ACT.Tanh, t, tmp.w, scale=0.5)
                            keep["t"] = ve.stt(t1_, t1_, 1.0, ps[:, :], ALU.add, ALU.mult, ta)
                            return [keep["t"]]
                        tb = ve.stt(t2_, t1_, 0.5, ps[:, :], ALU.mult, ALU.mult, t, keep["t"], tmp.w)
                        hi = OT.hi[:, b0:b0 + 2, :].rearrange("p a c -> p (a c)")
                        lo = OT.lo[:, b0:b0 + 2, :].rearrange("p a c -> p (a c)")
                        th = sc.act(hi, t2_, ACT.Copy, tb, OT.waits(b0, 2))
                        tl = po.tt(lo, t2_, hi.bitcast(F32), ALU.subtract, tb, th, OT.waits(b0, 2))
                        OT.write(b0, 2, [th, tl])
                        keep["r"] = [th, tl]
                        return [tb]
                    gemm(HT, 0, ("gu", l, v), D, "FF", ev)
                    tmp.release(keep["r"])
                if v == 1:
                    gb = bcast(l * 48 + 40, mod, mod_tok[l])
                if 0 < v < 11:
                    down(v - 1)
            nx, fr, sq, n4 = [], [[], []], [], smc(4)
            ws = [take(("dn", l, 10), ahead=False), take(("dn", l, 10), ahead=False)]
            for t in range(2):
                for n in range(2):
                    for kc in range(2):
                        s, wt = ws[kc]
                        b = 4 + kc
                        pe.wait(wt, OT.tok[b])
                        o = AB[t][:, n, :]
                        a = (OT.hi[:, b, t * P:t * P + P], OT.lo[:, b, t * P:t * P + P])
                        pe.mm(o, a[0], whi[:, s, n, :], False, False, skip=True)
                        pe.mm(o, a[0], wlo[:, s, n, :], False, False, skip=True)
                        tk = pe.mm(o, a[1], whi[:, s, n, :], False, kc == 1, skip=True, inc=(kc == 1))
                    fr[t] += residual(gb, n, nx, sq, n4)(t, AB[t][:, n, :], tk)
            for kc in range(2):
                spl_free[ws[kc][0]] = [tk]
                OT.free[4 + kc] = [tk]
                slots[t].ps_free = fr[t]
            xtok[:] = nx + sq
            xsq[:] = [n4, sq]
            gb.release(nx)

        for l in range(2):
            layer1(l)
        xtok[:] = final_norm(COL["g_final"], X)
        xsq[:] = squares(X, xtok)
        ada_sums()
        for l in range(4):
            gb = (swa_layer, gla_layer, fox_layer)[l % 3](l)
            nx, sq, n4 = [], [], smc(4)
            for u in range(2):
                gemm(OT, 0, ("wo2", l, u), D, "TT", residual(gb, u, nx, sq, n4), last=(u == 1))
            gb.release(nx)
            xtok[:] = nx + sq
            xsq[:] = [n4, sq]
            ffn(l)
        assert state["piece"] == len(stream) and not halves, (state, len(halves))
        tf = final_norm(COL["f_norm"], X)
        tout = load(sp, "out", out[0].rearrange("(t p) d -> p t d", p=P), X[:, :, :], tf)
        sp.wait(tout, scr[0])

        block = ctx.enter_context(nc.Block())

        def run(q):
            def f(eng):
                own = sems.get(q.key)
                for op in q.ops:
                    if op[0] == "wait":
                        eng.wait_ge(sems[op[1]], op[2])
                    elif op[0] == "dma":
                        eng.dma_start(op[1], op[2]).then_inc(sems[op[3]], 16)
                    else:
                        ins = op[1](eng)
                        if op[2]:
                            ins.then_inc(own, 1)
            return f

        block.tensor(run(pe))
        block.scalar(run(sc))
        block.vector(run(ve))
        block.gpsimd(run(po))
        block.sync(run(sp))


_INS = ['x', 'mem', 'g_norm', 'w_in', 'diff_lambda', 'w_mem_kv', 'g_mem', 'w_br_diff', 'w_br_dil', 'w_br_mem',
        'w_out', 'rel_bias', 'g_final', 'c_2', 'ada_w_2', 'ada_b_2', 'norm_gain_2', 'ffn_w_gu_2', 'ffn_w_down_2',
        'swa_w_in_2', 'swa_sinks_2', 'swa_w_o_2', 'gla_w_in_2', 'gla_w_gate_up_2', 'gla_b_gate_2',
        'gla_head_norm_2', 'gla_w_o_2', 'fox_w_in_2', 'fox_b_f_2', 'fox_w_o_2', 'final_norm_2']


def kernel(**inputs):
    import numpy as _np
    import concourse.bacc as _bacc
    from concourse.bass_utils import run_bass_kernel_spmd as _run

    nc = _bacc.Bacc("TRN2", target_bir_lowering=False, num_devices=1)
    arrays, ins, cst = {}, {}, {}
    for name in _INS:
        a = _np.ascontiguousarray(inputs[name])
        arrays[f"in_{name}"] = a
        ins[name] = nc.dram_tensor(f"in_{name}", a.shape, F32, kind="ExternalInput").ap()
    for name, a in constants().items():
        arrays[f"c_{name}"] = a
        cst[name] = nc.dram_tensor(f"c_{name}", a.shape, F32, kind="ExternalInput").ap()
    out = nc.dram_tensor("out", (1, T, D), F32, kind="ExternalOutput").ap()
    program(nc, ins, cst, out)
    r = _run(nc, [arrays], core_ids=[0])
    return r.results[0]["out"]
```
